# Optimizing a Trainium2 kernel written in Bass

```python
import jax, jax.numpy as jnp
from jax import lax
import numpy as np

D_MODEL = 2048
BATCH = 1
SEQ = 128
DEPTH = 1
DEC_BATCH = 1
DEC_SEQ = 128
PAST_LEN = 128

GRID_W = 64
NORM_EPS = 1e-6
M_HEADS = 4
M_QK = 128
M_V = 256
M_CHUNK = 64
M_QK_W = M_HEADS * M_QK
M_V_W = M_HEADS * M_V
M_GATES = 4 * M_HEADS
A_HEADS = 16
A_KV = 4
A_GROUP = A_HEADS // A_KV
A_HD = 64
A_Q_W = A_HEADS * A_HD
A_KV_W = A_KV * A_HD
WINDOW = 128
ROPE_THETA = 10000.0
D_FF = 5632
N_MOD = 9
IN_SIZES = (M_QK_W, M_QK_W, M_V_W, M_V_W, M_GATES, A_Q_W, A_KV_W, A_KV_W, D_MODEL, D_MODEL)
IN_COLS = 2 * M_QK_W + 2 * M_V_W + M_GATES + A_Q_W + 2 * A_KV_W + 2 * D_MODEL

kernel_name = 'hybrid_mlstm_swa_flow_step'

def rms_norm(x, w):
    xf = x.astype(jnp.float32)
    y = xf * lax.rsqrt(jnp.mean(xf * xf, axis=-1, keepdims=True) + NORM_EPS)
    return (y * w.astype(jnp.float32)).astype(x.dtype)

def modulation(cond, ada_w, ada_b):
    mod = jax.nn.silu(cond) @ ada_w + ada_b
    return jnp.split(mod[..., None, :], N_MOD, axis=-1)

def modulate(h, shift, scale):
    return h * (1 + scale) + shift

def swiglu(h, wi, wo):
    g, u = jnp.split(h @ wi, 2, axis=-1)
    return (jax.nn.silu(g) * u) @ wo

def ffn_sublayer(x, shift, scale, gate, norm_w, wi, wo):
    return x + 0.5 * gate * swiglu(modulate(rms_norm(x, norm_w), shift, scale), wi, wo)

def mixer_inputs(x, shift, scale, norm_w, w_in):
    z = modulate(rms_norm(x, norm_w), shift, scale) @ w_in
    idx, acc = [], 0
    for s in IN_SIZES[:-1]:
        acc += s
        idx.append(acc)
    return jnp.split(z, idx, axis=-1)

def rope_1d(x, pos):
    nf = x.shape[-1] // 2
    inv = ROPE_THETA ** (-jnp.arange(nf, dtype=jnp.float32) / nf)
    ang = pos.astype(jnp.float32)[:, None] * inv
    cos = jnp.cos(ang)[:, None, :]
    sin = jnp.sin(ang)[:, None, :]
    xf = x.astype(jnp.float32)
    x1, x2 = xf[..., :nf], xf[..., nf:]
    return jnp.concatenate([x1 * cos - x2 * sin, x1 * sin + x2 * cos], axis=-1).astype(x.dtype)

def axial_rope(x):
    n_tok = x.shape[1]
    rows = n_tok // GRID_W
    row = jnp.repeat(jnp.arange(rows), GRID_W)
    col = jnp.tile(jnp.arange(GRID_W), rows)
    half = A_HD // 2
    return jnp.concatenate([rope_1d(x[..., :half], row), rope_1d(x[..., half:], col)], axis=-1)

def mlstm_scan(q, k, v, ig, lf, C0, n0, m0):
    bsz, nh, n_tok, _ = q.shape
    nc = n_tok // M_CHUNK

    def chunks(a):
        return jnp.moveaxis(a.reshape(a.shape[:2] + (nc, M_CHUNK) + a.shape[3:]), 2, 0)

    tril = jnp.tril(jnp.ones((M_CHUNK, M_CHUNK), dtype=bool))

    def step(carry, inp):
        C, n, m = carry
        qc, kc, vc, ic, fc = inp
        b = jnp.cumsum(fc, axis=-1)
        dmat = jnp.where(tril, b[..., :, None] - b[..., None, :] + ic[..., None, :], -jnp.inf)
        inter = b + m[..., None]
        m_t = jnp.maximum(inter, jnp.max(dmat, axis=-1))
        s = jnp.einsum('bhtd,bhsd->bhts', qc, kc) * jnp.exp(dmat - m_t[..., None])
        decay = jnp.exp(inter - m_t)
        num = jnp.einsum('bhts,bhsv->bhtv', s, vc) + decay[..., None] * jnp.einsum('bhvd,bhtd->bhtv', C, qc)
        den = jnp.sum(s, axis=-1) + decay * jnp.einsum('bhd,bhtd->bht', n, qc)
        h = num / jnp.maximum(jnp.abs(den), jnp.exp(-m_t))[..., None]
        b_last = b[..., -1]
        g = b_last[..., None] - b + ic
        m_new = jnp.maximum(b_last + m, jnp.max(g, axis=-1))
        wk = jnp.exp(g - m_new[..., None])
        carry_decay = jnp.exp(b_last + m - m_new)
        C_new = carry_decay[..., None, None] * C + jnp.einsum('bhsv,bhsd->bhvd', vc * wk[..., None], kc)
        n_new = carry_decay[..., None] * n + jnp.einsum('bhs,bhsd->bhd', wk, kc)
        return (C_new, n_new, m_new), h

    (C, n, m), h = lax.scan(step, (C0, n0, m0), (chunks(q), chunks(k), chunks(v), chunks(ig), chunks(lf)))
    h = jnp.moveaxis(h, 0, 2).reshape(bsz, nh, n_tok, M_V)
    return h, C, n, m

def mlstm_branch(mq, mk, mv, mo, mg, gate_b, norm_w, C0, n0, m0):
    bsz, n_tok, _ = mq.shape
    f32 = jnp.float32

    def heads(a, d):
        return a.reshape(bsz, n_tok, M_HEADS, d).transpose(0, 2, 1, 3).astype(f32)

    q = heads(mq, M_QK) * (M_QK ** -0.5)
    k = heads(mk, M_QK)
    v = heads(mv, M_V)
    g = (mg.astype(f32) + gate_b.astype(f32)).transpose(0, 2, 1)
    i_f, f_f, i_b, f_b = jnp.split(g, 4, axis=1)
    C0, n0, m0 = C0.astype(f32), n0.astype(f32), m0.astype(f32)
    h_f, C_f, n_f, m_f = mlstm_scan(q, k, v, i_f, jax.nn.log_sigmoid(f_f), C0[:, 0], n0[:, 0], m0[:, 0])

    def rev(a):
        return jnp.flip(a, axis=2)

    h_b, C_b, n_b, m_b = mlstm_scan(rev(q), rev(k), rev(v), rev(i_b), rev(jax.nn.log_sigmoid(f_b)),
                                    C0[:, 1], n0[:, 1], m0[:, 1])
    h = h_f + rev(h_b)
    h = h * lax.rsqrt(jnp.mean(h * h, axis=-1, keepdims=True) + NORM_EPS)
    h = h.transpose(0, 2, 1, 3).reshape(bsz, n_tok, M_V_W) * norm_w.astype(f32)
    h = h * jax.nn.sigmoid(mo.astype(f32))
    states = (jnp.stack([C_f, C_b], axis=1), jnp.stack([n_f, n_b], axis=1), jnp.stack([m_f, m_b], axis=1))
    return h.astype(mq.dtype), states

def attn_qkv(aq, ak, av, q_norm_w, k_norm_w):
    bsz, n_tok, _ = aq.shape
    q = rms_norm(aq.reshape(bsz, n_tok, A_HEADS, A_HD), q_norm_w)
    k = rms_norm(ak.reshape(bsz, n_tok, A_KV, A_HD), k_norm_w)
    v = av.reshape(bsz, n_tok, A_KV, A_HD)
    return q, k, v

def context_attention(q, k, v, sink):
    bsz, n_tok = q.shape[:2]
    qg = q.reshape(bsz, n_tok, A_KV, A_GROUP, A_HD)
    s = jnp.einsum('btkgd,bskd->bkgts', qg, k, preferred_element_type=jnp.float32) * (A_HD ** -0.5)
    sk = jnp.broadcast_to(sink.astype(jnp.float32).reshape(1, A_KV, A_GROUP, 1, 1), s.shape[:-1] + (1,))
    p = jax.nn.softmax(jnp.concatenate([s, sk], axis=-1), axis=-1)[..., :-1]
    o = jnp.einsum('bkgts,bskd->btkgd', p.astype(v.dtype), v)
    return o.reshape(bsz, n_tok, A_Q_W)

def latent_attention(q, k, v, ck, cv, sink):
    bsz, n_tok = q.shape[:2]
    W = WINDOW
    nb = n_tok // W
    n_ctx = ck.shape[1]
    qb = q.reshape(bsz, nb, W, A_KV, A_GROUP, A_HD)
    pad = ((0, 0), (W, W), (0, 0), (0, 0))
    kb = jnp.pad(k, pad).reshape(bsz, nb + 2, W, A_KV, A_HD)
    vb = jnp.pad(v, pad).reshape(bsz, nb + 2, W, A_KV, A_HD)
    kw = jnp.concatenate([kb[:, :-2], kb[:, 1:-1], kb[:, 2:]], axis=2)
    vw = jnp.concatenate([vb[:, :-2], vb[:, 1:-1], vb[:, 2:]], axis=2)
    scale = A_HD ** -0.5
    s_loc = jnp.einsum('bnikgd,bnjkd->bkgnij', qb, kw, preferred_element_type=jnp.float32) * scale
    blk = jnp.arange(nb)[:, None, None]
    qpos = blk * W + jnp.arange(W)[None, :, None]
    kpos = (blk - 1) * W + jnp.arange(3 * W)[None, None, :]
    valid = (jnp.abs(kpos - qpos) <= WINDOW) & (kpos >= 0) & (kpos < n_tok)
    s_loc = jnp.where(valid, s_loc, -jnp.inf)
    s_ctx = jnp.einsum('bnikgd,bskd->bkgnis', qb, ck, preferred_element_type=jnp.float32) * scale
    sk = jnp.broadcast_to(sink.astype(jnp.float32).reshape(1, A_KV, A_GROUP, 1, 1, 1), s_loc.shape[:-1] + (1,))
    p = jax.nn.softmax(jnp.concatenate([s_loc, s_ctx, sk], axis=-1), axis=-1)
    p_loc = p[..., :3 * W].astype(v.dtype)
    p_ctx = p[..., 3 * W:3 * W + n_ctx].astype(v.dtype)
    o = jnp.einsum('bkgnij,bnjkd->bnikgd', p_loc, vw) + jnp.einsum('bkgnis,bskd->bnikgd', p_ctx, cv)
    return o.reshape(bsz, n_tok, A_Q_W)

def merge_branches(hm, ha, gm, ga, w_proj_m, w_proj_a, w_out):
    return (jax.nn.sigmoid(gm) * (hm @ w_proj_m) + jax.nn.sigmoid(ga) * (ha @ w_proj_a)) @ w_out

def setup_inputs(seed: int = 0) -> dict:
    key = jax.random.key(seed)
    ks = jax.random.split(key, 40)
    f32 = jnp.float32

    def nrm(k, shape, scale):
        return jax.random.normal(k, shape, f32) * scale

    gate_b = jnp.concatenate([
        nrm(ks[30], (DEPTH, M_HEADS), 0.1),
        3.0 + nrm(ks[31], (DEPTH, M_HEADS), 0.5),
        nrm(ks[32], (DEPTH, M_HEADS), 0.1),
        3.0 + nrm(ks[33], (DEPTH, M_HEADS), 0.5)], axis=-1)
    return {
        'x_prompt': nrm(ks[0], (BATCH, SEQ, D_MODEL), 1.0),
        'x_sample': nrm(ks[1], (DEC_BATCH, DEC_SEQ, D_MODEL), 1.0),
        'cache_attn_k': nrm(ks[2], (DEC_BATCH, DEPTH, PAST_LEN, A_KV, A_HD), 1.0),
        'cache_attn_v': nrm(ks[3], (DEC_BATCH, DEPTH, PAST_LEN, A_KV, A_HD), 1.0),
        'state_mlstm_C': nrm(ks[4], (DEC_BATCH, DEPTH, 2, M_HEADS, M_V, M_QK), 1.0),
        'state_mlstm_n': nrm(ks[5], (DEC_BATCH, DEPTH, 2, M_HEADS, M_QK), 1.0),
        'state_mlstm_m': nrm(ks[6], (DEC_BATCH, DEPTH, 2, M_HEADS), 1.0),
        'c': nrm(ks[7], (DEC_BATCH, D_MODEL), 1.0),
        'c_ctx': nrm(ks[8], (D_MODEL,), 1.0),
        'ada_w': nrm(ks[9], (DEPTH, D_MODEL, N_MOD * D_MODEL), D_MODEL ** -0.5),
        'ada_b': nrm(ks[10], (DEPTH, N_MOD * D_MODEL), 0.01),
        'norm_ffn1_w': 1.0 + nrm(ks[11], (DEPTH, D_MODEL), 0.05),
        'ffn1_wi': nrm(ks[12], (DEPTH, D_MODEL, 2 * D_FF), D_MODEL ** -0.5),
        'ffn1_wo': nrm(ks[13], (DEPTH, D_FF, D_MODEL), D_FF ** -0.5),
        'norm_mix_w': 1.0 + nrm(ks[14], (DEPTH, D_MODEL), 0.05),
        'w_in': nrm(ks[15], (DEPTH, D_MODEL, IN_COLS), D_MODEL ** -0.5),
        'mlstm_gate_b': gate_b,
        'mlstm_norm_w': 1.0 + nrm(ks[16], (DEPTH, M_V_W), 0.05),
        'attn_q_norm_w': 1.0 + nrm(ks[17], (DEPTH, A_HD), 0.05),
        'attn_k_norm_w': 1.0 + nrm(ks[18], (DEPTH, A_HD), 0.05),
        'attn_sink': nrm(ks[19], (DEPTH, A_HEADS), 0.5),
        'w_proj_m': nrm(ks[20], (DEPTH, M_V_W, D_MODEL), M_V_W ** -0.5),
        'w_proj_a': nrm(ks[21], (DEPTH, A_Q_W, D_MODEL), A_Q_W ** -0.5),
        'w_out': nrm(ks[22], (DEPTH, D_MODEL, D_MODEL), D_MODEL ** -0.5),
        'norm_ffn2_w': 1.0 + nrm(ks[23], (DEPTH, D_MODEL), 0.05),
        'ffn2_wi': nrm(ks[24], (DEPTH, D_MODEL, 2 * D_FF), D_MODEL ** -0.5),
        'ffn2_wo': nrm(ks[25], (DEPTH, D_FF, D_MODEL), D_FF ** -0.5),
    }

def reference(x_prompt, x_sample, cache_attn_k, cache_attn_v, state_mlstm_C, state_mlstm_n, state_mlstm_m,
              c, c_ctx, ada_w, ada_b, norm_ffn1_w, ffn1_wi, ffn1_wo, norm_mix_w, w_in, mlstm_gate_b,
              mlstm_norm_w, attn_q_norm_w, attn_k_norm_w, attn_sink, w_proj_m, w_proj_a, w_out,
              norm_ffn2_w, ffn2_wi, ffn2_wo):
    f32 = jnp.float32
    xc = x_prompt
    bp = x_prompt.shape[0]
    zero_C = jnp.zeros((bp, 2, M_HEADS, M_V, M_QK), f32)
    zero_n = jnp.zeros((bp, 2, M_HEADS, M_QK), f32)
    zero_m = jnp.zeros((bp, 2, M_HEADS), f32)
    ks_out, vs_out, Cs_out, ns_out, ms_out = [], [], [], [], []
    for l in range(DEPTH):
        sh1, sc1, g1, sh2, sc2, g2, sh3, sc3, g3 = modulation(c_ctx, ada_w[l], ada_b[l])
        xc = ffn_sublayer(xc, sh1, sc1, g1, norm_ffn1_w[l], ffn1_wi[l], ffn1_wo[l])
        mq, mk, mv, mo, mg, aq, ak, av, gm, ga = mixer_inputs(xc, sh2, sc2, norm_mix_w[l], w_in[l])
        hm, (C_l, n_l, m_l) = mlstm_branch(mq, mk, mv, mo, mg, mlstm_gate_b[l], mlstm_norm_w[l],
                                           zero_C, zero_n, zero_m)
        q, k, v = attn_qkv(aq, ak, av, attn_q_norm_w[l], attn_k_norm_w[l])
        ha = context_attention(q, k, v, attn_sink[l])
        xc = xc + g2 * merge_branches(hm, ha, gm, ga, w_proj_m[l], w_proj_a[l], w_out[l])
        xc = ffn_sublayer(xc, sh3, sc3, g3, norm_ffn2_w[l], ffn2_wi[l], ffn2_wo[l])
        ks_out.append(k)
        vs_out.append(v)
        Cs_out.append(C_l)
        ns_out.append(n_l)
        ms_out.append(m_l)
    y_prompt = xc
    new_attn_k = jnp.stack(ks_out, axis=1)
    new_attn_v = jnp.stack(vs_out, axis=1)
    new_mlstm_C = jnp.stack(Cs_out, axis=1)
    new_mlstm_n = jnp.stack(ns_out, axis=1)
    new_mlstm_m = jnp.stack(ms_out, axis=1)

    xs = x_sample
    for l in range(DEPTH):
        sh1, sc1, g1, sh2, sc2, g2, sh3, sc3, g3 = modulation(c, ada_w[l], ada_b[l])
        xs = ffn_sublayer(xs, sh1, sc1, g1, norm_ffn1_w[l], ffn1_wi[l], ffn1_wo[l])
        mq, mk, mv, mo, mg, aq, ak, av, gm, ga = mixer_inputs(xs, sh2, sc2, norm_mix_w[l], w_in[l])
        hm, _ = mlstm_branch(mq, mk, mv, mo, mg, mlstm_gate_b[l], mlstm_norm_w[l],
                             state_mlstm_C[:, l], state_mlstm_n[:, l], state_mlstm_m[:, l])
        q, k, v = attn_qkv(aq, ak, av, attn_q_norm_w[l], attn_k_norm_w[l])
        q = axial_rope(q)
        k = axial_rope(k)
        ha = latent_attention(q, k, v, cache_attn_k[:, l], cache_attn_v[:, l], attn_sink[l])
        xs = xs + g2 * merge_branches(hm, ha, gm, ga, w_proj_m[l], w_proj_a[l], w_out[l])
        xs = ffn_sublayer(xs, sh3, sc3, g3, norm_ffn2_w[l], ffn2_wi[l], ffn2_wo[l])
    y_sample = xs
    return (y_prompt, y_sample, new_attn_k, new_attn_v, new_mlstm_C, new_mlstm_n, new_mlstm_m)


_drawn_inputs = setup_inputs


def setup_inputs(seed=0):
    import zlib

    import numpy as np

    out = dict(_drawn_inputs(seed))
    spreads = {}
    factors = {'cache_attn_k': 2.826,
     'state_mlstm_n': 6.27,
     'state_mlstm_m': 2.808,
     'norm_ffn1_w': 2.733,
     'mlstm_norm_w': 6.427,
     'attn_q_norm_w': 8.0,
     'attn_sink': 64.0,
     'norm_ffn2_w': 3.252}
    for name, (base, spread) in spreads.items():
        noise = np.random.default_rng([zlib.crc32(name.encode()), seed]).standard_normal(out[name].shape)
        drawn = base * np.exp(spread * noise) if base else spread * noise
        out[name] = __import__('jax').numpy.asarray(drawn.astype(out[name].dtype))
    for name, factor in factors.items():
        out[name] = (out[name] * factor).astype(out[name].dtype)
    return out
```

```python
from contextlib import ExitStack

import numpy as np

import concourse.bass as bass
from concourse import mybir

F32 = mybir.dt.float32
F32R = mybir.dt.float32r
ALU = mybir.AluOpType
ACT = mybir.ActivationFunctionType
AX = mybir.AxisListType

P = 128
D = 2048
KD = D // P
GROUPS = 2
CTX, LAT = 0, 1
TOK = GROUPS * P
CH = 512
NCH = D // CH
D_FF = 5632
FCH = D_FF // CH
MH, MQK, MV = 4, 128, 256
AH, AKV, HD = 16, 4, 64
NMOD = 9
EPS = 1e-6
GRID_W = 64
NEG = -3.0e38

IN_GATES = 2 * MH * MQK + 2 * MH * MV
ZQ, ZK, ZV, ZO = 0, MH * MQK, 2 * MH * MQK, 2 * MH * MQK + MH * MV
ZAQ = IN_GATES
ZAK = ZAQ + AH * HD
ZAV = ZAK + AKV * HD
ZW = ZAV + AKV * HD
ZCH = ZW // CH
NG = 4 * MH
IN_GM = ZW + NG

U_F1 = 0
FFN_UNITS = 16 + (FCH - 1) * 24 + 8
U_IN = U_F1 + FFN_UNITS
U_MERGE = U_IN + 8 * ZCH
U_OUT = U_MERGE + 24 * NCH
U_F2 = U_OUT + 8 * NCH
U_END = U_F2 + FFN_UNITS
AHEAD = 3
RAW, SPL = 4, 4

SH1, SC1, G1, SH2, SC2, G2, SH3, SC3, G3 = range(NMOD)
ADA_PRE = 8

C_ID, C_TRI, C_MASK, C_COS, C_SIN, C_SEL, C_ONE = 0, 128, 384, 640, 704, 768, 770
C_W = 772


def shape_constants():
    c = np.zeros((P, C_W), np.float32)
    s, t = np.arange(P)[:, None], np.arange(P)[None, :]
    c[:, C_ID:C_ID + P] = s == t
    c[:, C_TRI:C_TRI + P] = s <= t
    c[:, C_TRI + P:C_TRI + 2 * P] = s >= t
    c[:, C_MASK:C_MASK + P] = np.where(s > t, 1e30, 0)
    c[:, C_MASK + P:C_MASK + 2 * P] = np.where(s < t, 1e30, 0)
    nf = HD // 4
    inv = np.float32(10000.0) ** (-np.arange(nf, dtype=np.float32) / np.float32(nf))
    for half, pos in enumerate((np.arange(P) // GRID_W, np.arange(P) % GRID_W)):
        ang = pos.astype(np.float32)[:, None] * inv
        o = half * 2 * nf
        c[:, C_COS + o:C_COS + o + nf] = c[:, C_COS + o + nf:C_COS + o + 2 * nf] = np.cos(ang)
        c[:, C_SIN + o:C_SIN + o + nf] = -np.sin(ang)
        c[:, C_SIN + o + nf:C_SIN + o + 2 * nf] = np.sin(ang)
    for j in range(4):
        c[32 * j, C_SEL] = c[32 * j + 1, C_SEL + 1] = 1
    c[:, C_ONE:C_ONE + 2] = 1
    return c


class Chain:

    def __init__(self, eng, sem):
        self.eng, self.sem, self.n = eng, sem, 0

    def __call__(self, *instructions):
        for ins in instructions:
            self.n += 1
            ins.then_inc(self.sem, 1)
        self.eng.wait_ge(self.sem, self.n)


def build(nc, I, O):
    ctx = ExitStack()
    with ctx:
        def sem(name):
            return ctx.enter_context(nc.semaphore(name))

        def sems(name, n):
            return [sem(f"{name}{i}") for i in range(n)]

        BASE = (nc.sbuf_base + 63) // 64 * 64
        top = [BASE]

        def place(name, shape, dt=F32, at=None):
            if at is not None:
                top[0] = at
            size = 4 * int(np.prod(shape[1:]))
            t = nc.alloc_sbuf_tensor_at(name, shape, dt, offset=top[0])
            top[0] += (size + 31) // 32 * 32
            assert top[0] <= 229344, (name, top[0])
            return t

        x = place("x", [P, GROUPS, D])
        xT_hi = place("xT_hi", [P, KD, TOK], F32R)
        xT_lo = place("xT_lo", [P, KD, TOK], F32R)
        raw_w = place("raw_w", [P, RAW, 4, CH])
        w_hi = place("w_hi", [P, SPL, 2, CH], F32R)
        w_lo = place("w_lo", [P, SPL, 2, CH], F32R)
        cst = place("cst", [P, C_W])
        adacols = place("adacols", [P, NMOD * KD, GROUPS])
        ctile = place("ctile", [P, KD, 32])
        normw = place("normw", [P, 3, KD])
        acol = place("acol", [P, KD, GROUPS])
        small = place("small", [P, 64])
        gates = place("gates", [P, GROUPS, NG])
        ROWS = top[0]
        colrows = place("colrows", [80, P])
        diag = place("diag", [P, GROUPS, P], at=ROWS)
        gate_rows = place("gate_rows", [2 * KD, 2, P], at=ROWS)
        SLOT = top[0]
        acc = place("acc", [P, GROUPS, D])
        AFTER_ACC = top[0]
        h = place("h", [P, GROUPS, CH])
        sg = place("sg", [P, GROUPS, CH])
        hT_hi = place("hT_hi", [P, 4, TOK], F32R)
        hT_lo = place("hT_lo", [P, 4, TOK], F32R)
        xm = place("xm", [P, KD, TOK], at=AFTER_ACC)
        Z = place("Z", [P, GROUPS, ZW], at=SLOT)
        SCR = top[0]
        ada_w_sb = place("ada_w_sb", [P, 4, 4, CH])
        AFTER_ADA = top[0]
        gate_bc = place("gate_bc", [P, GROUPS, D], at=SCR + 16384)
        y_tmp = place("y_tmp", [P, GROUPS, CH], at=SCR)
        top[0] = AFTER_ADA
        ada_bias = place("ada_bias", [P, 2, CH])
        ada_rows_sb = place("ada_rows_sb", [P, CH])
        wg_raw = place("wg_raw", [P, KD, NG])
        wg_hi = place("wg_hi", [P, KD, NG], F32R)
        wg_lo = place("wg_lo", [P, KD, NG], F32R)
        gateb = place("gateb", [P, NG])
        END = top[0]
        cache_k = place("cache_k", [P, AKV * HD])
        cache_v = place("cache_v", [P, AKV * HD])
        m_normw = place("m_normw", [P, MH * MV])
        qk_w = place("qk_w", [P, 2, HD])
        sink = place("sink", [P, AH])
        m0_bc = place("m0_bc", [P, 2, MH])
        m0_row = place("m0_row", [40, 1])
        NC = 2 * GROUPS * MH
        absf = place("absf", [P, NC])
        lf = place("lf", [P, 2, GROUPS * MH])
        bcol = place("bcol", [P, 2, GROUPS * MH])
        apad = place("apad", [P, 2, 32])
        mcol = place("mcol", [P, 2, GROUPS * MH])
        mt = place("mt", [P, 2, GROUPS * MH])
        exp_negm = place("exp_negm", [P, NC])
        decay = place("decay", [P, 2, MH])
        wk = place("wk", [P, MH, 2])
        den = place("den", [P, NC])
        scan = [place(f"scan{i}", [40, 2 * P]) for i in range(2)]
        n0_rows = place("n0_rows", [2 * MH, P])
        n0T = place("n0T", [P, 2 * MH])
        stat = place("stat", [P, 3, 2 * (AH + AKV)])
        row_sum = place("row_sum", [P, 2 * AH])
        neg_max = place("neg_max", [P, 2 * AH])
        num = place("num", [P, NC, MV + 1], at=SCR)
        c_raw = place("c_raw", [P, 2 * MH * 2, MQK], at=SCR)
        CT = place("CT", [P, 2 * MH, MV], at=SCR + 16480)
        c_new = place("c_new", [P, 2, MH * 2, MQK], at=SCR + 16480)
        qkT = place("qkT", [P, 4, MH, P])
        decays = place("decays", [P, 2, MH, P])
        sT = place("sT", [P, 2, MH, P])
        v_wk = place("v_wk", [P, 2, MH, MV], at=SCR + 16480 + 16384)
        assert top[0] <= END
        k_dup = place("k_dup", [P, 3, AKV, 2, HD], at=SCR)
        kTz_ctx = place("kTz_ctx", [P, AKV, 2, P])
        kTz_lat = place("kTz_lat", [P, AKV, 2, 2 * P])
        qT = place("qT", [P, GROUPS, AH // 2, P])
        A_TMP = top[0]
        prob = place("prob", [P, 2, CH])
        probT = place("probT", [P, 2, CH])
        sq = place("sq", [P, GROUPS, ZAV - ZAQ], at=A_TMP)
        assert top[0] <= END
        hcT_hi = place("hcT_hi", [P, KD, TOK], F32R, at=SCR)
        hcT_lo = place("hcT_lo", [P, KD, TOK], F32R)
        sgm = place("sgm", [P, GROUPS, CH], at=SLOT)
        sga = place("sga", [P, GROUPS, CH])
        mix = place("mix", [P, GROUPS, D], at=SLOT + 16384)
        n_new = place("n_new", [2, MH * P], at=SCR + 16480 + 8192)
        ps = nc.alloc_psum_tensor("ps", [P, 8, CH], F32)

        gate_dram = nc.dram_tensor("gate_dram", (3, KD, GROUPS, P), F32).ap()
        ident = cst[:, C_ID:C_ID + P]

        raw_landed = sems("raw_landed", RAW)
        hi_ready, lo_ready, units_done = sem("hi_ready"), sem("lo_ready"), sem("units_done")
        cst_landed, rows_landed, x_landed = sem("cst_landed"), sem("rows_landed"), sem("x_landed")
        cols_ps, cond_silu, normw_ready, zeroed = sem("cols_ps"), sem("cond_silu"), sem("normw_ready"), sem("zeroed")
        ada_landed, bias_landed = sems("ada_landed", 4), sems("bias_landed", 2)
        ada_used, ada_acc_done, ada_rows_done = sem("ada_used"), sem("ada_acc_done"), sem("ada_rows_done")
        ada_sel_done, ada_cols_done = sem("ada_sel_done"), sem("ada_cols_done")
        sumsq_ready, var_ready, root_ready, diag_ready = sem("sumsq_ready"), sem("var_ready"), sem("root_ready"), sem("diag_ready")
        bias_zeroed, xm_act, acol_ready = sem("bias_zeroed"), sem("xm_act"), sem("acol_ready")
        gate_rows_ps, gate_rows_ready, gate_stored, gate_landed = (
            sem("gate_rows_ps"), sem("gate_rows_ready"), sem("gate_stored"), sem("gate_landed"))
        norm_ps, xm_ready, xT_hi_ready, xT_lo_ready = sem("norm_ps"), sem("xm_ready"), sem("xT_hi_ready"), sem("xT_lo_ready")
        silu_done, h_done, hT_ps, hT_hi_ready, hT_lo_ready, acc_done = (
            sem("silu_done"), sem("h_done"), sem("hT_ps"), sem("hT_hi_ready"), sem("hT_lo_ready"), sem("acc_done"))
        x_updated = sem("x_updated")
        dve_chain, act_chain = sem("dve_chain"), sem("act_chain")
        out_landed = sem("out_landed")
        wg_landed, wg_hi_ready, wg_ready, gates_ps, gates_ready = (
            sem("wg_landed"), sem("wg_hi_ready"), sem("wg_ready"), sem("gates_ps"), sem("gates_ready"))
        z_copied, misc_landed = sem("z_copied"), sem("misc_landed")
        absf_ready, softplus_ready, lf_ready, b_ps, a_ready, aT_ps, scan_done, mT_ps = (
            sem("absf_ready"), sem("softplus_ready"), sem("lf_ready"), sem("b_ps"), sem("a_ready"),
            sem("aT_ps"), sem("scan_done"), sem("mT_ps"))
        m_ready, m_last_ps, wk_arg, wk_ready, mt_ready, exps_ready = (
            sem("m_ready"), sem("m_last_ps"), sem("wk_arg"), sem("wk_ready"), sem("mt_ready"), sem("exps_ready"))
        c_landed, qkT_ps, qkT_copied, CT_ps, CT_copied = (
            sem("c_landed"), sem("qkT_ps"), sem("qkT_copied"), sem("CT_ps"), sem("CT_copied"))
        qkT_copied_act, CT_copied_act = sem("qkT_copied_act"), sem("CT_copied_act")
        qk_ps, mb_ps, decays_ready, sT_ready, sv_ps, sv_copied, inter_ps, inter_added = (
            sem("qk_ps"), sem("mb_ps"), sem("decays_ready"), sem("sT_ready"), sem("sv_ps"), sem("sv_copied"),
            sem("inter_ps"), sem("inter_added"))
        v_wk_ready, state_ps, state_copied, state_copied_act = (
            sem("v_wk_ready"), sem("state_ps"), sem("state_copied"), sem("state_copied_act"))
        h_var, h_root, sig_o, hm_ready = sem("h_var"), sem("h_root"), sem("sig_o"), sem("hm_ready")
        kT_zeroed, qk_var, qk_root, k_normed, rope_done, k_dup_ready = (
            sem("kT_zeroed"), sem("qk_var"), sem("qk_root"), sem("k_normed"), sem("rope_done"), sem("k_dup_ready"))
        atT_ps, qT_copied, kT_copied = sem("atT_ps"), sem("qT_copied"), sem("kT_copied")
        score_ps, neg_max_ready, prob_ready, probT_ps, probT_ready, pv_done, sink_exp, ha_ready = (
            sem("score_ps"), sem("neg_max_ready"), sem("prob_ready"), sem("probT_ps"), sem("probT_ready"),
            sem("pv_done"), sem("sink_exp"), sem("ha_ready"))
        hcT_ps, hcT_hi_ready, hcT_lo_ready = sem("hcT_ps"), sem("hcT_hi_ready"), sem("hcT_lo_ready")
        sgm_ready, sga_ready, gm_used, ga_used, mix_ready = (
            sem("sgm_ready"), sem("sga_ready"), sem("gm_used"), sem("ga_used"), sem("mix_ready"))
        mixT_ps, mixT_hi_ready, mixT_lo_ready = sem("mixT_ps"), sem("mixT_hi_ready"), sem("mixT_lo_ready")
        state_stored, kv_stored, sink_arg = sem("state_stored"), sem("kv_stored"), sem("sink_arg")

        def at_least(eng, s, v):
            if not isinstance(v, int) or v > 0:
                eng.wait_ge(s, v)

        blk = ctx.enter_context(nc.Block())

        @blk.sync
        def _(sp):
            sp.dma_start(cst[:], I["consts"]).then_inc(cst_landed, 16)
            for n, name in enumerate(("c_ctx", "c", "norm_ffn1_w", "norm_mix_w", "norm_ffn2_w")):
                src = I[name].rearrange("(k p) -> k p", p=P) if len(I[name].shape) == 1 else \
                    I[name].rearrange("a (k p) -> (a k) p", p=P)
                sp.dma_start(colrows[16 * n:16 * n + 16, :], src).then_inc(rows_landed, 16)
            sp.wait_ge(ada_used, 8)
            sp.dma_start(x[:, CTX, :], I["x_prompt"][0]).then_inc(x_landed, 16)
            sp.dma_start(x[:, LAT, :], I["x_sample"][0]).then_inc(x_landed, 16)
            sp.wait_ge(ada_used, 4 * ADA_PRE - 6)

            def tile(ts, tx, src):
                at_least(sp, lo_ready, 2 * (ts + tx) - 2 * RAW + 2)
                sp.dma_start(raw_w[:, ts % RAW, :, :], src).then_inc(raw_landed[ts % RAW], 16)

            def rows(w, q):
                return w[0].rearrange("(q k p) n -> q p k n", k=4, p=P)[q]

            def ffn(f, t0):
                wi, wo = I[f"ffn{f + 1}_wi"], I[f"ffn{f + 1}_wo"]

                def ffn_in(i, ts, tx):
                    for part in range(2):
                        for q in range(4):
                            tile(ts + 4 * part + q, tx, rows(wi, q)[:, :, bass.ds(i * CH + part * D_FF, CH)])

                def ffn_out(j, ts, tx):
                    src = wo[0].rearrange("(q k p) n -> p q k n", k=4, p=P)
                    for n in range(NCH):
                        s = src[:, bass.ds(j, 1), :, n * CH:(n + 1) * CH]
                        tile(ts + n, tx, s.rearrange("p a k n -> p (a k) n"))

                ffn_in(0, t0, 0)
                with sp.Fori(1, FCH) as i:
                    ffn_in(i, t0 + 8, (i - 1) * 12)
                    ffn_out(i - 1, t0 + 16, (i - 1) * 12)
                ffn_out(FCH - 1, t0 + 8 + 12 * (FCH - 1), 0)

            ffn(0, U_F1 // 2)
            w_in = I["w_in"]
            with sp.Fori(0, 3) as i:
                for c in range(2):
                    for q in range(4):
                        tile(U_IN // 2 + 4 * c + q, i * 8, rows(w_in, q)[:, :, bass.ds(i * (2 * CH) + c * CH, CH)])
            for c in range(6, ZCH):
                for q in range(4):
                    tile(U_IN // 2 + 4 * c + q, 0, rows(w_in, q)[:, :, c * CH + NG:(c + 1) * CH + NG])
            with sp.Fori(0, NCH) as n:
                for q in range(4):
                    tile(U_MERGE // 2 + q, n * 12, rows(w_in, q)[:, :, bass.ds(n * CH + IN_GM, CH)])
                for q in range(4):
                    tile(U_MERGE // 2 + 4 + q, n * 12, rows(w_in, q)[:, :, bass.ds(n * CH + IN_GM + D, CH)])
                for q in range(2):
                    tile(U_MERGE // 2 + 8 + q, n * 12, rows(I["w_proj_m"], q)[:, :, bass.ds((n + n) * (CH // 2), CH)])
                for q in range(2):
                    tile(U_MERGE // 2 + 10 + q, n * 12, rows(I["w_proj_a"], q)[:, :, bass.ds((n + n) * (CH // 2), CH)])
            with sp.Fori(0, NCH) as n:
                for q in range(4):
                    tile(U_OUT // 2 + q, n * 4, rows(I["w_out"], q)[:, :, bass.ds(n * CH, CH)])
            ffn(1, U_F2 // 2)
            for n in range(NCH):
                sp.wait_ge(x_updated, 2 * NCH + n + 1)
                for g, name in enumerate(("y_prompt", "y_sample")):
                    sp.dma_start(O[name][0][:, n * CH:(n + 1) * CH], x[:, g, n * CH:(n + 1) * CH]).then_inc(out_landed, 16)
            sp.wait_ge(out_landed, 16 * 2 * NCH)
            sp.wait_ge(state_stored, 16 * 5)
            sp.wait_ge(kv_stored, 16 * 2)

        @blk.gpsimd
        def _(pool):
            pool.memset(acc[:], 0.0).then_inc(acc_done, 1)
            pool.wait_ge(ada_used, 4 * ADA_PRE + 4)
            def all_rows(ap, n):
                return ap.broadcast_to([P, n])

            pool.dma_start(wg_raw[:], I["w_in"][0].rearrange("(k p) n -> p k n", p=P)[:, :, IN_GATES:IN_GATES + NG]).then_inc(wg_landed, 16)
            for dst, src in (
                    (gateb[:], all_rows(I["mlstm_gate_b"], NG)),
                    (cache_k[:], I["cache_attn_k"][0, 0].rearrange("s k d -> s (k d)")),
                    (cache_v[:], I["cache_attn_v"][0, 0].rearrange("s k d -> s (k d)")),
                    (m_normw[:], all_rows(I["mlstm_norm_w"], MH * MV)),
                    (qk_w[:, 0, :], all_rows(I["attn_q_norm_w"], HD)),
                    (qk_w[:, 1, :], all_rows(I["attn_k_norm_w"], HD)),
                    (sink[:], all_rows(I["attn_sink"], AH)),
                    (m0_bc[:].rearrange("p d h -> p (d h)"),
                     all_rows(I["state_mlstm_m"][0].rearrange("a d h -> a (d h)"), 2 * MH)),
                    (n0_rows[:], I["state_mlstm_n"][0, 0].rearrange("d h k -> (d h) k"))):
                pool.dma_start(dst, src).then_inc(misc_landed, 16)
            pool.wait_ge(zeroed, 1)
            for d in range(2):
                pool.dma_start(m0_row[32 * d + MH:32 * d + 2 * MH, :],
                             I["state_mlstm_m"][0, 0, d].rearrange("(h a) -> h a", a=1)).then_inc(misc_landed, 16)


            def gate_load(r):
                for g in range(GROUPS):
                    row = gate_dram[r].rearrange("(a k) g p -> g a k p", a=1)[g]
                    pool.dma_start(gate_bc[:, g, :].rearrange("q (k p) -> q k p", p=P),
                                   row.broadcast_to([P, KD, P])).then_inc(gate_landed, 16)

            def gate_store(r, at):
                pool.dma_start(gate_dram[r].rearrange("k g p -> (k g) p"), gate_rows[:, at, :]).then_inc(gate_stored, 16)

            pool.wait_ge(gate_rows_ready, 1)
            gate_store(0, 0)
            pool.wait_ge(gate_stored, 16)
            pool.wait_ge(ada_used, 4 * (ADA_PRE + 2 * (FCH - 1)))
            gate_load(0)
            pool.wait_ge(gate_rows_ready, 2)
            gate_store(1, 0)
            gate_store(2, 1)
            pool.wait_ge(ada_used, NMOD * KD)
            pool.dma_start(c_raw[:], I["state_mlstm_C"][0, 0].rearrange("d h (a p) k -> p (d h a) k", p=P)).then_inc(c_landed, 16)
            pool.wait_ge(mt_ready, 1)
            pool.dma_start(O["new_mlstm_m"][0, 0:1, 0, :], mt[P - 1:P, 0, 0:MH]).then_inc(state_stored, 16)
            pool.dma_start(O["new_mlstm_m"][0, 0:1, 1, :], mt[0:1, 1, 0:MH]).then_inc(state_stored, 16)
            pool.wait_ge(state_copied, 3)
            pool.wait_ge(state_copied_act, 2)
            for d in range(2):
                pool.dma_start(O["new_mlstm_C"][0, 0, d].rearrange("h (a p) k -> p (h a) k", p=P),
                               c_new[:, d, :, :]).then_inc(state_stored, 16)
            pool.dma_start(O["new_mlstm_n"][0, 0].rearrange("d h k -> d (h k)"), n_new[:]).then_inc(state_stored, 16)
            pool.wait_ge(state_stored, 80)
            pool.wait_ge(hm_ready, 1)
            pool.memset(kTz_ctx[:], 0.0).then_inc(kT_zeroed, 1)
            pool.memset(kTz_lat[:], 0.0).then_inc(kT_zeroed, 1)
            pool.wait_ge(k_normed, 1)
            pool.dma_start(O["new_attn_k"][0, 0].rearrange("s k d -> s (k d)"), Z[:, CTX, ZAK:ZAV]).then_inc(kv_stored, 16)
            pool.dma_start(O["new_attn_v"][0, 0].rearrange("s k d -> s (k d)"), Z[:, CTX, ZAV:ZW]).then_inc(kv_stored, 16)
            pool.wait_ge(mix_ready, NCH)
            pool.memset(acc[:], 0.0).then_inc(acc_done, 1)
            pool.wait_ge(units_done, U_OUT)
            pool.wait_ge(gate_stored, 48)
            gate_load(1)
            pool.wait_ge(x_updated, 2 * NCH)
            gate_load(2)

        @blk.tensor
        def _(pe):
            def ada_acc(c):
                at_least(pe, ada_rows_done, c)
                for q in range(4):
                    pe.wait_ge(ada_landed[q], 16 * (c + 1))
                    for j in range(4):
                        mm = pe.matmul(ps[32 * j:32 * j + 32, 6, :], ctile[:, 4 * q + j, :],
                                       ada_w_sb[:, q, j, :], start=(q == 0), stop=(q == 3))
                    mm.then_inc(ada_used, 1)
                    last = mm

            def ada_sel(c):
                pe.wait_ge(ada_rows_done, c + 1)
                at_least(pe, ada_cols_done, c)
                for b in range(4):
                    mm = pe.matmul(ps[:, 7, 2 * b:2 * b + 2], ada_rows_sb[:, b * P:(b + 1) * P],
                                   cst[:, C_SEL:C_SEL + 2], start=True, stop=True)
                mm.then_inc(ada_sel_done, 1)

            def norm(s, banks=range(8)):
                pe.wait_ge(diag_ready, s + 1)
                for j in banks:
                    for b in range(2):
                        for g in range(GROUPS):
                            k = 2 * j + b
                            mm = pe.matmul(ps[:, j, b * TOK + g * P:b * TOK + (g + 1) * P],
                                           x[:, g, k * P:(k + 1) * P], diag[:, g, :], start=True, stop=True)
                    mm.then_inc(norm_ps, 1)

            def unit(us, ux, hi, lo, kb, banks, first, last):
                pe.wait_ge(lo_ready, us + ux + 1)
                slot = us % SPL
                for kk in range(2):
                    for g in range(GROUPS):
                        a_hi = hi[:, kb + kk, g * P:(g + 1) * P]
                        a_lo = lo[:, kb + kk, g * P:(g + 1) * P]
                        out = ps[:, banks + g, :]
                        pe.matmul(out, a_hi, w_hi[:, slot, kk, :], start=(first and kk == 0), stop=False)
                        pe.matmul(out, a_hi, w_lo[:, slot, kk, :], start=False, stop=False)
                        mm = pe.matmul(out, a_lo, w_hi[:, slot, kk, :], start=False, stop=(last and kk == 1))
                mm.then_inc(units_done, 1)

            def x_chunk(us, ux, banks, between=None, stage=None):
                for k in range(8):
                    if stage is not None:
                        pe.wait_ge(xT_lo_ready, 8 * stage + max(k + 1, 2))
                    unit(us + k, ux, xT_hi, xT_lo, 2 * k, banks, k == 0, k == 7)
                    if between:
                        between(k)

            def gate_T(vecs):
                for n, vec in enumerate(vecs):
                    mm = pe.transpose(ps[0:2 * KD, 7, n * P:(n + 1) * P],
                                      adacols[:, vec * KD:(vec + 1) * KD, :].rearrange("p k g -> p (k g)"), ident)
                mm.then_inc(gate_rows_ps, 1)

            def ffn(f, u0, stage):
                def ffn_in(i, us, ux, ada=None):
                    def g_between(k):
                        if ada is not None and k == 3:
                            ada_acc(ada)
                        if ada is not None and k == 6:
                            ada_sel(ada)

                    def u_between(k):
                        if ada is not None and k == 3:
                            ada_acc(ada + 1)
                        if ada is not None and k == 6:
                            ada_sel(ada + 1)

                    first = isinstance(i, int)
                    if not first:
                        pe.wait_ge(silu_done, FCH * f + i)
                    x_chunk(us, ux, 0, g_between, stage if first else None)
                    if not first:
                        pe.wait_ge(h_done, FCH * f + i)
                        pe.wait_ge(acc_done, 45 * f + 4 * i - 3)
                    x_chunk(us + 8, ux, 2, u_between)

                def ffn_out(j, us, ux, epilogue=False):
                    for n in range(NCH):
                        banks = 4 if n % 2 == 0 else 2
                        if n == 0:
                            pe.wait_ge(hT_lo_ready, FCH * f + j + 1)
                        elif n == 1:
                            if epilogue:
                                pe.wait_ge(acc_done, 45 * f + 4 * j + 1)
                            else:
                                pe.wait_ge(h_done, FCH * f + j + 2)
                        else:
                            pe.wait_ge(acc_done, 45 * f + 4 * j + n)
                        for k in range(2):
                            unit(us + 2 * n + k, ux, hT_hi, hT_lo, 2 * k, banks, k == 0, k == 1)

                def h_transposes(i):
                    pe.wait_ge(h_done, FCH * f + i + 1)
                    if not isinstance(i, int):
                        pe.wait_ge(acc_done, 45 * f + 4 * i)
                    for b in range(4):
                        for g in range(GROUPS):
                            mm = pe.transpose(ps[:, 4 + b // 2, (b % 2) * TOK + g * P:(b % 2) * TOK + (g + 1) * P],
                                              h[:, g, b * P:(b + 1) * P], ident)
                    mm.then_inc(hT_ps, 1)

                ffn_in(0, u0, 0)
                h_transposes(0)
                with pe.Fori(1, FCH) as i:
                    ffn_in(i, u0 + 16, (i - 1) * 24, 2 * i + ADA_PRE - 2 if f == 0 else None)
                    ffn_out(i - 1, u0 + 32, (i - 1) * 24)
                    h_transposes(i)
                if f == 0:
                    pe.wait_ge(ada_cols_done, ADA_PRE + 2 * (FCH - 1))
                    gate_T((G1,))
                ffn_out(FCH - 1, u0 + 16 + 24 * (FCH - 1), 0, True)

            pe.wait_ge(cst_landed, 16)
            pe.wait_ge(rows_landed, 80)
            pe.transpose(ps[:, 0, 0:80], colrows[:, :], cst[0:80, C_ID:C_ID + 80]).then_inc(cols_ps, 1)
            pe.wait_ge(cond_silu, 1)
            for c in range(4):
                ada_acc(c)
                ada_sel(c)
            norm(0, range(6))
            with pe.Fori(4, ADA_PRE) as c:
                ada_acc(c)
                ada_sel(c)
            pe.wait_ge(ada_cols_done, ADA_PRE)
            norm(0, range(6, 8))
            ffn(0, U_F1, 0)

            norm(1)
            def z_pair(c, ux):
                for m in range(2):
                    at_least(pe, z_copied, c + m - 1)

                    def between(k):
                        if k == 3:
                            ada_acc(c + m + 4 * G2 + 8)
                        if k == 6:
                            ada_sel(c + m + 4 * G2 + 8)

                    x_chunk(U_IN + 8 * m, ux, 2 * m, between, 1 if isinstance(c, int) and m == 0 else None)

            z_pair(0, 0)
            pe.wait_ge(wg_ready, 1)
            for g in range(GROUPS):
                for k in range(KD):
                    a_hi, a_lo = xT_hi[:, k, g * P:(g + 1) * P], xT_lo[:, k, g * P:(g + 1) * P]
                    out = ps[:, 4 + g, 0:NG]
                    pe.matmul(out, a_hi, wg_hi[:, k, :], start=(k == 0), stop=False)
                    pe.matmul(out, a_hi, wg_lo[:, k, :], start=False, stop=False)
                    mm = pe.matmul(out, a_lo, wg_hi[:, k, :], start=False, stop=(k == KD - 1))
                mm.then_inc(gates_ps, 1)
            with pe.Fori(1, 4) as i:
                z_pair(2 * i, i * 16)
            pe.wait_ge(ada_cols_done, NMOD * 4)
            gate_T((G2, G3))
            pe.wait_ge(z_copied, 7)
            x_chunk(U_IN + 64, 0, 0)

            pe.wait_ge(lf_ready, 1)
            for d in range(2):
                mm = pe.matmul(ps[:, 4, 8 * d:8 * d + 8], cst[:, C_TRI + d * P:C_TRI + (d + 1) * P], lf[:, d, :],
                               start=True, stop=True)
            mm.then_inc(b_ps, 1)
            pe.wait_ge(a_ready, 1)
            pe.transpose(ps[0:40, 5, 0:P], apad[:].rearrange("p d c -> p (d c)")[:, 0:40], ident).then_inc(aT_ps, 1)
            pe.wait_ge(z_copied, ZCH)
            for n in range(4):
                for hd in range(MH):
                    o = (ZQ, ZK)[n // 2] + hd * MQK
                    mm = pe.transpose(ps[:, n, hd * P:(hd + 1) * P], Z[:, n % 2, o:o + MQK], ident)
                mm.then_inc(qkT_ps, 1)
            pe.wait_ge(scan_done, 14)
            pe.transpose(ps[:, 4, 0:40], scan[1][:, P // 2:P // 2 + P], cst[0:40, C_ID:C_ID + 40]).then_inc(mT_ps, 1)
            pe.wait_ge(m_ready, 1)
            for d in range(2):
                last = (P - 1, 0)[d]
                mm = pe.matmul(ps[:, 5, 4 * d:4 * d + 4], cst[:, C_ID + last:C_ID + last + 1].to_broadcast([P, P]),
                               mcol[:, d, 0:MH], start=True, stop=True)
            mm.then_inc(m_last_ps, 1)
            pe.wait_ge(wk_arg, 2)
            pe.wait_ge(qkT_copied, 2)
            pe.wait_ge(qkT_copied_act, 2)
            pe.wait_ge(c_landed, 16)
            for n in range(4):
                for j in range(4):
                    mm = pe.transpose(ps[:, 2 + n, j * P:(j + 1) * P], c_raw[:, 4 * n + j, :], ident)
                mm.then_inc(CT_ps, 1)
            for g in range(GROUPS):
                for hd in range(MH):
                    mm = pe.matmul(ps[:, g, hd * P:(hd + 1) * P], qkT[:, 2 + g, hd, :], qkT[:, g, hd, :],
                                   start=True, stop=True)
                mm.then_inc(qk_ps, 1)
            pe.wait_ge(misc_landed, 16 * 11)
            pe.transpose(ps[:, 6, 0:2 * MH], n0_rows[:], cst[0:2 * MH, C_ID:C_ID + 2 * MH]).then_inc(CT_ps, 1)
            pe.wait_ge(CT_copied, 3)
            pe.wait_ge(CT_copied_act, 2)

            def m_rows(i):
                d, g = i // 2, i % 2
                at_least(pe, decays_ready, i - 1)
                for hd in range(MH):
                    out = ps[:, 2 + i % 2, hd * P:(hd + 1) * P]
                    pe.matmul(out, ident, cst[:, C_MASK + d * P:C_MASK + (d + 1) * P], start=True, stop=False)
                    mm = pe.matmul(out, mcol[:, d, g * MH + hd:g * MH + hd + 1].to_broadcast([P, P]), ident,
                                   start=False, stop=True)
                mm.then_inc(mb_ps, 1)

            def sv(i):
                d, g = i // 2, i % 2
                pe.wait_ge(sT_ready, i + 1)
                for hd in range(MH):
                    n = 4 * i + hd
                    at_least(pe, sv_copied, n - 1)
                    pe.matmul(ps[:, 4 + n % 2, 0:MV], sT[:, i % 2, hd, :], Z[:, g, ZV + hd * MV:ZV + (hd + 1) * MV],
                              start=True, stop=True)
                    pe.matmul(ps[:, 4 + n % 2, MV:MV + 1], sT[:, i % 2, hd, :], cst[:, C_ONE:C_ONE + 1],
                              start=True, stop=True).then_inc(sv_ps, 1)

            for i in range(5):
                if i < 4:
                    m_rows(i)
                if i:
                    sv(i - 1)
            for n in range(2 * MH):
                d, hd = n // MH, n % MH
                at_least(pe, inter_added, n - 1)
                pe.matmul(ps[:, 6 + n % 2, 0:MV], qkT[:, LAT, hd, :], CT[:, n, :], start=True, stop=True)
                pe.matmul(ps[:, 6 + n % 2, MV:MV + 1], qkT[:, LAT, hd, :], n0T[:, n:n + 1],
                          start=True, stop=True).then_inc(inter_ps, 1)
            pe.wait_ge(v_wk_ready, 2)
            pe.wait_ge(sv_copied, 16)
            for n in range(4):
                for j in range(4):
                    d, hd, a = n // 2, 2 * (n % 2) + j // 2, j % 2
                    mm = pe.matmul(ps[:, 2 + n, j * P:(j + 1) * P], v_wk[:, d, hd, a * P:(a + 1) * P],
                                   Z[:, CTX, ZK + hd * MQK:ZK + (hd + 1) * MQK], start=True, stop=True)
                mm.then_inc(state_ps, 1)
            for hd in range(MH):
                mm = pe.matmul(ps[0:2, 0, hd * P:(hd + 1) * P], wk[:, hd, :], Z[:, CTX, ZK + hd * MQK:ZK + (hd + 1) * MQK],
                               start=True, stop=True)
            mm.then_inc(state_ps, 1)

            pe.wait_ge(rope_done, 1)
            pe.wait_ge(state_copied, 3)
            pe.wait_ge(state_copied_act, 2)
            for n in range(4):
                g = n // 2
                for j in range(4):
                    o = ZAQ + (4 * (n % 2) + j) * P
                    mm = pe.transpose(ps[:, n, j * P:(j + 1) * P], Z[:, g, o:o + P], ident)
                mm.then_inc(atT_ps, 1)
            pe.wait_ge(k_dup_ready, 3)
            for n in range(3):
                pe.wait_ge(qT_copied, n + 1)
                for kv in range(AKV):
                    mm = pe.transpose(ps[:, n, kv * P:(kv + 1) * P], k_dup[:, n, kv, :, :].rearrange("p a d -> p (a d)"), ident)
                mm.then_inc(atT_ps, 1)

            def scores(i):
                at_least(pe, prob_ready, i - 1)
                if i < 4:
                    for j in range(2):
                        mm = pe.matmul(ps[:, i % 2, 256 * j:256 * (j + 1)], qT[:, CTX, 2 * i + j, :],
                                       kTz_ctx[:, i, :, :], start=True, stop=True)
                else:
                    mm = pe.matmul(ps[:, i % 2, :], qT[:, LAT, i - 4, :], kTz_lat[:, (i - 4) // 2, :, :],
                                   start=True, stop=True)
                mm.then_inc(score_ps, 1)

            def prob_transposes(i):
                pe.wait_ge(prob_ready, i + 1)
                at_least(pe, probT_ready, i - 1)
                for j in range(4):
                    mm = pe.transpose(ps[:, 2 + i % 2, j * P:(j + 1) * P], prob[:, i % 2, j * P:(j + 1) * P], ident)
                mm.then_inc(probT_ps, 1)

            def values(i):
                pe.wait_ge(probT_ready, i + 1)
                if i == 4:
                    pe.wait_ge(ha_ready, 1)
                for c in range(4 if i < 4 else 2):
                    hd = 4 * i + c if i < 4 else 2 * (i - 4) + c
                    out = ps[:, 4 + hd // 8, (hd % 8) * HD:(hd % 8 + 1) * HD]
                    v = ZAV + hd // 4 * HD
                    if i < 4:
                        mm = pe.matmul(out, probT[:, i % 2, c * P:(c + 1) * P], Z[:, CTX, v:v + HD], start=True, stop=True)
                    else:
                        o = 2 * c * P
                        pe.matmul(out, probT[:, i % 2, o:o + P], Z[:, LAT, v:v + HD], start=True, stop=False)
                        mm = pe.matmul(out, probT[:, i % 2, o + P:o + 2 * P], cache_v[:, v - ZAV:v - ZAV + HD],
                                       start=False, stop=True)
                mm.then_inc(pv_done, 1)

            pe.wait_ge(kT_copied, 3)
            pe.wait_ge(qT_copied, 4)
            for i in range(14):
                if i < 12:
                    scores(i)
                if 1 <= i <= 12:
                    prob_transposes(i - 1)
                if i >= 2:
                    values(i - 2)

            def blocks_T(at, done):
                for j in range(8):
                    for b in range(2):
                        for g in range(GROUPS):
                            mm = pe.transpose(ps[:, j, b * TOK + g * P:b * TOK + (g + 1) * P], at(g, 2 * j + b), ident)
                    mm.then_inc(done, 1)

            pe.wait_ge(ha_ready, 2)
            pe.wait_ge(hm_ready, 1)
            blocks_T(lambda g, k: Z[:, g, ZV + k * P:ZV + (k + 1) * P] if k < 8 else Z[:, g, ZAQ + (k - 8) * P:ZAQ + (k - 7) * P],
                     hcT_ps)
            pe.wait_ge(hcT_lo_ready, 8)

            def merge(n, ux):
                at_least(pe, sgm_ready, n)
                x_chunk(U_MERGE, ux, 0)
                at_least(pe, sga_ready, n)
                x_chunk(U_MERGE + 8, ux, 2)
                at_least(pe, gm_used, n)
                for k in range(4):
                    unit(U_MERGE + 16 + k, ux, hcT_hi, hcT_lo, 2 * k, 4, k == 0, k == 3)
                at_least(pe, mix_ready, n)
                for k in range(4):
                    unit(U_MERGE + 20 + k, ux, hcT_hi, hcT_lo, 8 + 2 * k, 6, k == 0, k == 3)

            merge(0, 0)
            with pe.Fori(1, NCH) as n:
                merge(n, n * 24)
            pe.wait_ge(mix_ready, NCH)
            blocks_T(lambda g, k: mix[:, g, k * P:(k + 1) * P], mixT_ps)
            for n in range(NCH):
                if n >= 2:
                    pe.wait_ge(x_updated, NCH + n - 1)
                for k in range(8):
                    if n == 0:
                        pe.wait_ge(mixT_lo_ready, min(k + 2, 8))
                    unit(U_OUT + 8 * n + k, 0, xT_hi, xT_lo, 2 * k, 2 * (n % 2), k == 0, k == 7)
            norm(2)
            ffn(1, U_F2, 2)

        @blk.scalar
        def _(act):
            chain = Chain(act, act_chain)

            def split(us, ux, n=1):
                if isinstance(ux, int) and us + ux >= U_END:
                    return
                slot = (us // 2) % RAW
                if us % 2 == 0:
                    act.wait_ge(raw_landed[slot], 16 * (us // 2 // RAW + 1) + ux * 2)
                at_least(act, units_done, us + ux - SPL + 1)
                half = us % 2
                act.copy(w_hi[:, us % SPL, :, :], raw_w[:, slot, 2 * half:2 * half + 2, :]).then_inc(hi_ready, 1)

            def ada_load(c, par, tiles=range(4)):
                src = I["ada_b"][0:1, bass.ds(c * CH, CH)].broadcast_to([GROUPS, CH])
                if 0 in tiles:
                    at_least(act, ada_rows_done, c - 1)
                    act.dma_start(ada_bias[0:GROUPS, par, :], src).then_inc(bias_landed[par], 16)
                for q in tiles:
                    w = I["ada_w"][0].rearrange("(q k p) n -> q p k n", k=4, p=P)[q]
                    at_least(act, ada_used, 4 * c + q - 3)
                    act.dma_start(ada_w_sb[:, q, :, :], w[:, :, bass.ds(c * CH, CH)]).then_inc(ada_landed[q], 16)

            def sumsq(s, n):
                at_least(act, x_updated, NCH * (s - 1) + n + 1)
                at_least(act, sumsq_ready, 2 * (NCH * s + n) if n else 0)
                for g in range(GROUPS):
                    act.activation(sg[:, g, :], x[:, g, n * CH:(n + 1) * CH], ACT.Square,
                                   accum_out=small[:, 4 * g + n:4 * g + n + 1]).then_inc(sumsq_ready, 1)

            def root(s):
                act.wait_ge(var_ready, s + 1)
                act.activation(small[:, 12:14], small[:, 10:12], ACT.Sqrt).then_inc(root_ready, 1)

            def norm(s, sh):
                act.wait_ge(acol_ready, s + 1)
                for j in range(8):
                    if j % 2:
                        act.wait_ge(norm_ps, 8 * s + j + 1)
                        for b in range(2):
                            for g in range(GROUPS):
                                k = 2 * j + b
                                ins = act.activation(xm[:, k, g * P:(g + 1) * P], ps[:, j, b * TOK + g * P:b * TOK + (g + 1) * P],
                                                     ACT.Identity, scale=acol[:, k, g:g + 1],
                                                     bias=adacols[:, sh * KD + k, g:g + 1])
                        ins.then_inc(xm_act, 1)
                        act.wait_ge(xm_act, 4 * s + j // 2 + 1)
                    else:
                        act.wait_ge(xm_ready, 4 * s + j // 2 + 1)
                    act.copy(xT_hi[:, 2 * j:2 * j + 2, :], xm[:, 2 * j:2 * j + 2, :]).then_inc(xT_hi_ready, 1)

            def ffn(f, u0):
                def hT_hi_of(i):
                    act.wait_ge(hT_ps, FCH * f + i + 1)
                    act.copy(hT_hi[:].rearrange("p (a b) t -> p a (b t)", a=2), ps[:, 4:6, :]).then_inc(hT_hi_ready, 1)

                def ffn_in(i, us, ux, ada=None, last=False):
                    first = isinstance(i, int) and i == 0
                    for k in range(16):
                        split(us + k + AHEAD, ux)
                        if k == 0 and not first:
                            hT_hi_of(i - 1)
                        if ada is not None and k == 5:
                            ada_load(ada + 1, 1)
                        if ada is not None and k == 13:
                            ada_load(ada + 2, 0, range(2) if last else range(4))
                        if k == 7:
                            act.wait_ge(units_done, us + ux + 8)
                            if not first:
                                act.wait_ge(h_done, FCH * f + i)
                            act.activation(sg[:], ps[:, 0:2, :], ACT.Silu).then_inc(silu_done, 1)

                def step(i, ux, last=False):
                    ffn_in(i, u0 + 16, ux, 2 * i + ADA_PRE - 2 if f == 0 else None, last)
                    for k in range(8):
                        split(u0 + 32 + k + AHEAD, ux)

                ffn_in(0, u0, 0)
                with act.Fori(1, FCH - 1) as i:
                    step(i, (i - 1) * 24)
                step(FCH - 1, (FCH - 2) * 24, True)
                for k in range(8):
                    split(u0 + 16 + 24 * (FCH - 1) + k + AHEAD, 0)
                    if k == 0:
                        hT_hi_of(FCH - 1)
                        act.wait_ge(h_done, FCH * f + FCH)
                    if f == 0 and k in (4, 6):
                        sumsq(1, k // 2 - 2)

            act.wait_ge(bias_zeroed, 1)
            ada_load(0, 0)
            act.wait_ge(cols_ps, 1)
            act.activation(ctile[:, :, 0:GROUPS].rearrange("p k g -> p g k"),
                           ps[:, 0, 0:GROUPS * KD].rearrange("p (g k) -> p g k", g=GROUPS),
                           ACT.Silu).then_inc(cond_silu, 1)
            for c in range(1, 4):
                ada_load(c, c % 2)
            act.wait_ge(x_landed, 32)
            for n in range(NCH):
                sumsq(0, n)
            root(0)
            with act.Fori(2, ADA_PRE // 2) as i:
                ada_load(2 * i, 0)
                ada_load(2 * i + 1, 1)
            for u in range(AHEAD):
                split(u, 0)
            ada_load(ADA_PRE, 0)
            norm(0, SH1)
            ffn(0, U_F1)
            sumsq(1, 2)
            sumsq(1, 3)
            root(1)
            ada_load(ADA_PRE + 2 * (FCH - 1), 0, range(2, 4))

            norm(1, SH2)
            act.wait_ge(wg_landed, 16)
            act.copy(wg_hi[:], wg_raw[:]).then_inc(wg_hi_ready, 1)

            def z_pair(c, ux, last=False):
                for m in range(2):
                    for k in range(8):
                        split(U_IN + 8 * m + k + AHEAD, ux)
                        if k == 5 and not (last and m):
                            ada_load(c + m + 4 * G2 + 9, 1 - m)
                        if k == 7:
                            act.wait_ge(units_done, U_IN + 8 * m + 8 + ux)
                            act.copy(Z[:, :, bass.ds((c + m) * CH, CH)], ps[:, 2 * m:2 * m + 2, :]).then_inc(z_copied, 1)

            z_pair(0, 0)
            with act.Fori(1, 3) as i:
                z_pair(2 * i, i * 16)
            z_pair(6, 48, True)
            for k in range(8):
                split(U_IN + 64 + k + AHEAD, 0)
            act.wait_ge(units_done, U_MERGE)
            act.copy(Z[:, :, ZW - CH:ZW], ps[:, 0:2, :]).then_inc(z_copied, 1)

            act.wait_ge(absf_ready, 1)
            chain(act.activation(exp_negm[:], absf[:], ACT.Exp, scale=-1.0))
            act.activation(den[:], exp_negm[:], ACT.Ln, bias=1.0).then_inc(softplus_ready, 1)
            for n in range(2):
                act.wait_ge(qkT_ps, n + 1)
                act.copy(qkT[:, n, :, :].rearrange("p h t -> p (h t)"), ps[:, n, :]).then_inc(qkT_copied_act, 1)
            act.wait_ge(mt_ready, 1)
            act.activation(exp_negm[:], mt[:].rearrange("p d c -> p (d c)"), ACT.Exp, scale=-1.0).then_inc(exps_ready, 1)
            act.wait_ge(wk_arg, 2)
            act.activation(decay[:], decay[:], ACT.Exp).then_inc(exps_ready, 1)
            act.activation(wk[:], wk[:], ACT.Exp).then_inc(wk_ready, 1)
            for n in range(2):
                act.wait_ge(CT_ps, n + 1)
                act.copy(CT[:, 2 * n:2 * n + 2, :].rearrange("p a v -> p (a v)"), ps[:, 2 + n, :]).then_inc(CT_copied_act, 1)

            def decays_of(i):
                d, g = i // 2, i % 2
                act.wait_ge(mb_ps, i + 1)
                at_least(act, sT_ready, i - 1)
                for hd in range(MH):
                    ins = act.activation(decays[:, i % 2, hd, :], ps[:, 2 + i % 2, hd * P:(hd + 1) * P], ACT.Exp,
                                         bias=apad[:, d, g * MH + hd:g * MH + hd + 1], scale=-1.0)
                ins.then_inc(decays_ready, 1)

            def sv_copy(i):
                if i == 0:
                    act.wait_ge(CT_ps, 4)
                for hd in range(MH):
                    n = 4 * i + hd
                    act.wait_ge(sv_ps, n + 1)
                    act.copy(num[:, n, :], ps[:, 4 + n % 2, 0:MV + 1]).then_inc(sv_copied, 1)

            for i in range(5):
                if i < 4:
                    decays_of(i)
                if i:
                    sv_copy(i - 1)
            for n in range(2):
                act.wait_ge(state_ps, n + 1)
                act.wait_ge(inter_added, 8)
                act.copy(c_new[:, 0, 4 * n:4 * n + 4, :].rearrange("p a k -> p (a k)"), ps[:, 2 + n, :]).then_inc(state_copied_act, 1)
            act.activation(Z[:, :, ZO:ZO + MH * MV], Z[:, :, ZO:ZO + MH * MV], ACT.Sigmoid).then_inc(sig_o, 1)
            act.wait_ge(h_var, 1)
            act.activation(stat[:, 1, 0:2 * MH], stat[:, 0, 0:2 * MH], ACT.Sqrt).then_inc(h_root, 1)

            act.wait_ge(qk_var, 1)
            act.activation(stat[:, 1, :], stat[:, 0, :], ACT.Sqrt).then_inc(qk_root, 1)
            for n in range(4):
                act.wait_ge(atT_ps, n + 1)
                act.copy(qT[:, n // 2, 4 * (n % 2):4 * (n % 2) + 4, :].rearrange("p a t -> p (a t)"),
                         ps[:, n, :]).then_inc(qT_copied, 1)

            for i in range(12):
                act.wait_ge(neg_max_ready, i + 1)
                at_least(act, probT_ps, i - 1)
                heads, keys = (4, P) if i < 4 else (2, 2 * P)
                for c in range(heads):
                    col = 4 * i + c if i < 4 else AH + 2 * (i - 4) + c
                    ins = act.activation(prob[:, i % 2, c * keys:(c + 1) * keys], ps[:, i % 2, c * keys:(c + 1) * keys],
                                         ACT.Exp, bias=neg_max[:, col:col + 1], accum_out=row_sum[:, col:col + 1])
                ins.then_inc(prob_ready, 1)
                if i in (5, 11):
                    act.wait_ge(sink_arg, i // 6 + 1)
                    act.activation(stat[:, 1, 0:AH], stat[:, 0, 0:AH], ACT.Exp).then_inc(sink_exp, 1)

            def blocks_hi(hi, src_ps, done):
                for j in range(8):
                    act.wait_ge(src_ps, j + 1)
                    act.copy(hi[:, 2 * j:2 * j + 2, :].rearrange("p a t -> p (a t)"), ps[:, j, :]).then_inc(done, 1)

            blocks_hi(hcT_hi, hcT_ps, hcT_hi_ready)

            def merge(n, ux):
                for k in range(24):
                    split(U_MERGE + k + AHEAD, ux)
                    if k == 7:
                        act.wait_ge(units_done, U_MERGE + 8 + ux)
                        at_least(act, mix_ready, n)
                        act.activation(sgm[:], ps[:, 0:2, :], ACT.Sigmoid).then_inc(sgm_ready, 1)
                    if k == 15:
                        act.wait_ge(units_done, U_MERGE + 16 + ux)
                        act.activation(sga[:], ps[:, 2:4, :], ACT.Sigmoid).then_inc(sga_ready, 1)

            merge(0, 0)
            with act.Fori(1, NCH) as n:
                merge(n, n * 24)
            blocks_hi(xT_hi, mixT_ps, mixT_hi_ready)
            for k in range(8 * NCH):
                split(U_OUT + k + AHEAD, 0)
                if k % 8 == 4 and k > 8:
                    sumsq(2, k // 8 - 1)
            sumsq(2, 3)
            root(2)
            norm(2, SH3)
            ffn(1, U_F2)

        @blk.vector
        def _(dve):
            chain = Chain(dve, dve_chain)

            def split(us, ux):
                if isinstance(ux, int) and us + ux >= U_END:
                    return
                slot, half = (us // 2) % RAW, us % 2
                dve.wait_ge(hi_ready, us + ux + 1)
                dve.tensor_tensor(w_lo[:, us % SPL, :, :], raw_w[:, slot, 2 * half:2 * half + 2, :],
                                  w_hi[:, us % SPL, :, :].bitcast(F32), ALU.subtract).then_inc(lo_ready, 1)

            def ada_rows(c, par, uses):
                dve.wait_ge(ada_used, 4 * c + 4)
                dve.wait_ge(bias_landed[par], uses)
                at_least(dve, ada_sel_done, c)
                dve.tensor_tensor(ada_rows_sb[:], ps[:, 6, :], ada_bias[:, par, :], ALU.add).then_inc(ada_rows_done, 1)

            def gates_copy(vecs, n):
                dve.wait_ge(gate_rows_ps, n)
                dve.tensor_copy(gate_rows[:, 0:len(vecs), :], ps[0:2 * KD, 7, 0:P * len(vecs)].rearrange("k (v p) -> k v p", p=P)
                                ).then_inc(gate_rows_ready, 1)

            def ada_cols(c):
                dve.wait_ge(ada_sel_done, c + 1)
                dve.tensor_copy(adacols[:, bass.ds(4 * c, 4), :].rearrange("p a g -> p (a g)"),
                                ps[:, 7, 0:8]).then_inc(ada_cols_done, 1)

            def scale(s, sc):
                dve.wait_ge(ada_cols_done, 4 * (sc + 1))
                dve.scalar_tensor_tensor(
                    acol[:], adacols[:, sc * KD:(sc + 1) * KD, :], 1.0,
                    normw[:, s, :].unsqueeze(2).to_broadcast([P, KD, GROUPS]), ALU.add, ALU.mult).then_inc(acol_ready, 1)

            def rms(s):
                dve.wait_ge(sumsq_ready, 2 * NCH * (s + 1))
                chain(dve.tensor_reduce(small[:, 8:10], small[:, 0:8].rearrange("p (g n) -> p g n", g=GROUPS), AX.X, ALU.add))
                dve.tensor_scalar(small[:, 10:12], small[:, 8:10], 1.0 / D, EPS, ALU.mult, ALU.add).then_inc(var_ready, 1)
                dve.wait_ge(root_ready, s + 1)
                chain(dve.reciprocal(small[:, 14:16], small[:, 12:14]))
                for g in range(GROUPS):
                    ins = dve.tensor_scalar(diag[:, g, :], ident, small[:, 14 + g:15 + g], None, ALU.mult)
                ins.then_inc(diag_ready, 1)

            def norm(s, sh):
                dve.wait_ge(acol_ready, s + 1)

                def modulate(j):
                    dve.wait_ge(norm_ps, 8 * s + j + 1)
                    for b in range(2):
                        for g in range(GROUPS):
                            k = 2 * j + b
                            ins = dve.tensor_scalar(xm[:, k, g * P:(g + 1) * P], ps[:, j, b * TOK + g * P:b * TOK + (g + 1) * P],
                                                    acol[:, k, g:g + 1], adacols[:, sh * KD + k, g:g + 1], ALU.mult, ALU.add)
                    ins.then_inc(xm_ready, 1)

                def low(j):
                    dve.wait_ge(xT_hi_ready, 8 * s + j + 1)
                    dve.tensor_tensor(xT_lo[:, 2 * j:2 * j + 2, :], xm[:, 2 * j:2 * j + 2, :],
                                      xT_hi[:, 2 * j:2 * j + 2, :].bitcast(F32), ALU.subtract).then_inc(xT_lo_ready, 1)

                modulate(0)
                for j in range(8):
                    if j % 2 == 0 and j < 6:
                        modulate(j + 2)
                    low(j)

            def ffn(f, u0):
                def hT_lo_of(i):
                    dve.wait_ge(hT_hi_ready, FCH * f + i + 1)
                    dve.tensor_tensor(hT_lo[:].rearrange("p (a b) t -> p a (b t)", a=2), ps[:, 4:6, :],
                                      hT_hi[:].bitcast(F32).rearrange("p (a b) t -> p a (b t)", a=2),
                                      ALU.subtract).then_inc(hT_lo_ready, 1)

                def ffn_in(i, us, ux, ada=None):
                    for k in range(16):
                        split(us + k + AHEAD, ux)
                        if k == 0 and not isinstance(i, int):
                            hT_lo_of(i - 1)
                        if ada is not None:
                            if k == 4:
                                ada_rows(ada, 0, 8 * ada + 16)
                            if k == 7:
                                ada_cols(ada)
                            if k == 12:
                                ada_rows(ada + 1, 1, 8 * ada + 16)
                            if k == 15:
                                ada_cols(ada + 1)
                        if k == 15:
                            dve.wait_ge(units_done, us + ux + 16)
                            dve.wait_ge(silu_done, FCH * f + i + 1)
                            if not isinstance(i, int):
                                dve.wait_ge(hT_ps, FCH * f + i)
                            dve.tensor_tensor(h[:], sg[:], ps[:, 2:4, :], ALU.mult).then_inc(h_done, 1)

                def ffn_out(j, us, ux, epilogue=False):
                    for k in range(8):
                        split(us + k + AHEAD, ux)
                        if k == 0 and epilogue:
                            hT_lo_of(j)
                            if f == 0:
                                gates_copy((G1,), 1)
                        if k % 2:
                            n = k // 2
                            a = acc[:, :, n * CH:(n + 1) * CH]
                            dve.wait_ge(units_done, us + ux + k + 1)
                            dve.wait_ge(acc_done, 45 * f + 4 * j + n + 1)
                            banks = 4 if n % 2 == 0 else 2
                            dve.tensor_tensor(a, a, ps[:, banks:banks + 2, :], ALU.add).then_inc(acc_done, 1)
                            if epilogue:
                                xx = x[:, :, n * CH:(n + 1) * CH]
                                dve.wait_ge(gate_landed, 32 * (2 * f + 1))
                                dve.wait_ge(acc_done, 45 * f + 4 * j + n + 2)
                                chain(dve.tensor_tensor(a, a, gate_bc[:, :, n * CH:(n + 1) * CH], ALU.mult))
                                dve.scalar_tensor_tensor(xx, a, 0.5, xx, ALU.mult, ALU.add).then_inc(x_updated, 1)

                ffn_in(0, u0, 0)
                with dve.Fori(1, FCH) as i:
                    ffn_in(i, u0 + 16, (i - 1) * 24, 2 * i + ADA_PRE - 2 if f == 0 else None)
                    ffn_out(i - 1, u0 + 32, (i - 1) * 24)
                ffn_out(FCH - 1, u0 + 16 + 24 * (FCH - 1), 0, True)

            dve.memset(ctile[:], 0.0)
            dve.memset(ada_bias[:], 0.0).then_inc(bias_zeroed, 1)
            dve.memset(m0_row[:], 0.0)
            dve.memset(apad[:], 0.0)
            for t in scan:
                ins = dve.memset(t[:], NEG)
            ins.then_inc(zeroed, 1)
            dve.wait_ge(cols_ps, 1)
            dve.wait_ge(cond_silu, 1)
            chain(dve.tensor_copy(normw[:].rearrange("p s k -> p (s k)"), ps[:, 0, 32:80]))
            for c in range(4):
                ada_rows(c, c % 2, 16 * (c // 2 + 1))
                ada_cols(c)
            rms(0)
            with dve.Fori(2, ADA_PRE // 2) as i:
                ada_rows(2 * i, 0, 16 * i + 16)
                ada_cols(2 * i)
                ada_rows(2 * i + 1, 1, 16 * i + 16)
                ada_cols(2 * i + 1)
            for u in range(AHEAD):
                split(u, 0)
            scale(0, SC1)
            norm(0, SH1)
            ffn(0, U_F1)
            scale(1, SC2)
            rms(1)

            norm(1, SH2)
            dve.wait_ge(wg_hi_ready, 1)
            dve.tensor_tensor(wg_lo[:], wg_raw[:], wg_hi[:].bitcast(F32), ALU.subtract).then_inc(wg_ready, 1)

            def z_pair(c, ux):
                for m in range(2):
                    a = c + m + 4 * G2 + 8
                    for k in range(8):
                        split(U_IN + 8 * m + k + AHEAD, ux)
                        if k == 4:
                            ada_rows(a, m, 8 * c + 16 * (2 * G2 + 5))
                        if k == 7:
                            ada_cols(a)

            z_pair(0, 0)
            dve.wait_ge(misc_landed, 16 * 11)
            for g in range(GROUPS):
                dve.wait_ge(gates_ps, g + 1)
                ins = dve.tensor_tensor(gates[:, g, :], ps[:, 4 + g, 0:NG], gateb[:], ALU.add)
                chain(ins)
            gate = gates[:].rearrange("p g (d i h) -> p i d g h", d=2, i=2)
            i_pre, f_pre = gate[:, 0], gate[:, 1]

            def by_dgh(t):
                return t.rearrange("p d (g h) -> p d g h", g=GROUPS)

            absf_v = absf[:].rearrange("p (d g h) -> p d g h", d=2, g=GROUPS)
            for d in range(2):
                ins = dve.scalar_tensor_tensor(absf_v[:, d], f_pre[:, d], -1.0, f_pre[:, d], ALU.mult, ALU.max)
            ins.then_inc(absf_ready, 1)
            with dve.Fori(1, 4) as i:
                z_pair(2 * i, i * 16)
            gates_copy((G2, G3), 2)
            for k in range(8):
                split(U_IN + 64 + k + AHEAD, 0)

            dve.wait_ge(softplus_ready, 1)
            den_v = den[:].rearrange("p (d g h) -> p d g h", d=2, g=GROUPS)
            for d in range(2):
                ins = dve.scalar_tensor_tensor(by_dgh(lf[:])[:, d], f_pre[:, d], 0.0, den_v[:, d], ALU.min, ALU.subtract)
            ins.then_inc(lf_ready, 1)
            dve.wait_ge(b_ps, 1)
            b_v = ps[:, 4, 0:NC].rearrange("p (d g h) -> p d g h", d=2, g=GROUPS)
            dve.tensor_copy(bcol[:].rearrange("p d c -> p (d c)"), ps[:, 4, 0:NC])
            for d in range(2):
                ins = dve.tensor_tensor(by_dgh(apad[:, :, 0:GROUPS * MH])[:, d], i_pre[:, d], b_v[:, d], ALU.subtract)
            ins.then_inc(a_ready, 1)
            dve.wait_ge(aT_ps, 1)
            H = P // 2
            chain(dve.tensor_scalar(scan[0][:, H:H + P], ps[0:40, 5, 0:P], m0_row[:, 0:1], None, ALU.max))
            for n in range(7):
                src, dst, s = scan[n % 2], scan[(n + 1) % 2], 1 << n
                for r, to in ((slice(0, 8), -s), (slice(32, 40), s)):
                    dve.tensor_tensor(dst[r, H:H + P], src[r, H:H + P], src[r, H + to:H + to + P], ALU.max).then_inc(scan_done, 1)
                dve.wait_ge(scan_done, 2 * (n + 1))
            for n in range(2, 4):
                dve.wait_ge(qkT_ps, n + 1)
                dve.tensor_copy(qkT[:, n, :, :].rearrange("p h t -> p (h t)"), ps[:, n, :]).then_inc(qkT_copied, 1)
            dve.wait_ge(mT_ps, 1)
            chain(dve.tensor_copy(mcol[:, 0, :], ps[:, 4, 0:8]), dve.tensor_copy(mcol[:, 1, :], ps[:, 4, 32:40]))
            dve.tensor_tensor(decay[:], m0_bc[:], mcol[:, :, MH:2 * MH], ALU.subtract).then_inc(m_ready, 1)
            dve.tensor_tensor(mt[:], bcol[:], mcol[:], ALU.add).then_inc(mt_ready, 1)
            dve.wait_ge(m_last_ps, 1)
            for d in range(2):
                dve.tensor_tensor(wk[:, :, d], apad[:, d, 0:MH], ps[:, 5, 4 * d:4 * d + 4], ALU.subtract).then_inc(wk_arg, 1)
            for n in range(2, 4):
                dve.wait_ge(CT_ps, n + 1)
                dve.tensor_copy(CT[:, 2 * n:2 * n + 2, :].rearrange("p a v -> p (a v)"), ps[:, 2 + n, :]).then_inc(CT_copied, 1)
            dve.wait_ge(CT_ps, 5)
            dve.tensor_copy(n0T[:], ps[:, 6, 0:2 * MH]).then_inc(CT_copied, 1)
            dve.wait_ge(exps_ready, 2)
            chain(dve.tensor_scalar(decay[:], decay[:], MQK ** -0.5, None, ALU.mult))
            for i in range(4):
                d, g = i // 2, i % 2
                dve.wait_ge(decays_ready, i + 1)
                dve.wait_ge(qk_ps, g + 1)
                at_least(dve, sv_ps, 4 * (i - 1))
                dve.scalar_tensor_tensor(sT[:, i % 2, :, :].rearrange("p h t -> p (h t)"), ps[:, g, :], MQK ** -0.5,
                                         decays[:, i % 2, :, :].rearrange("p h t -> p (h t)"),
                                         ALU.mult, ALU.mult).then_inc(sT_ready, 1)
            for n in range(2 * MH):
                d, hd = n // MH, n % MH
                col = d * GROUPS * MH + MH + hd
                dve.wait_ge(inter_ps, n + 1)
                dve.wait_ge(sv_copied, col + 1)
                dve.scalar_tensor_tensor(num[:, col, :], ps[:, 6 + n % 2, 0:MV + 1], decay[:, d, hd:hd + 1],
                                         num[:, col, :], ALU.mult, ALU.add).then_inc(inter_added, 1)
            dve.wait_ge(wk_ready, 1)
            dve.wait_ge(sv_ps, 16)
            for d in range(2):
                dve.tensor_tensor(v_wk[:, d, :, :], Z[:, CTX, ZV:ZV + MH * MV].rearrange("p (h v) -> p h v", h=MH),
                                  wk[:, :, d:d + 1].to_broadcast([P, MH, MV]), ALU.mult).then_inc(v_wk_ready, 1)
            den_col = num[:, :, MV:MV + 1].rearrange("p c a -> p (c a)")
            dve.wait_ge(inter_added, 8)
            dve.wait_ge(exps_ready, 1)
            chain(dve.scalar_tensor_tensor(den[:], den_col, -1.0, den_col, ALU.mult, ALU.max))
            chain(dve.tensor_tensor(den[:], den[:], exp_negm[:], ALU.max))
            chain(dve.reciprocal(den[:], den[:]))
            v_num = num[:, :, 0:MV]
            chain(dve.tensor_tensor(v_num, v_num, den[:].unsqueeze(2).to_broadcast([P, NC, MV]), ALU.mult))
            for n in range(2):
                dve.wait_ge(state_ps, 3 + n)
                dve.tensor_copy(c_new[:, 1, 4 * n:4 * n + 4, :].rearrange("p a k -> p (a k)"), ps[:, 4 + n, :]).then_inc(state_copied, 1)
            dve.wait_ge(state_ps, 5)
            dve.tensor_copy(n_new[:], ps[0:2, 0, :]).then_inc(state_copied, 1)
            Zh = Z[:, :, ZV:ZV + MH * MV].rearrange("p g (h v) -> p g h v", h=MH)
            Zo = Z[:, :, ZO:ZO + MH * MV]
            fw = num[:, 0:8, 0:MV].rearrange("p (g h) v -> p g h v", g=GROUPS)
            bw = num[:, 8:16, 0:MV].rearrange("p (g h) v -> p g h v", g=GROUPS)
            for g in range(GROUPS):
                chain(dve.tensor_tensor(Zh[:, g], fw[:, g], bw[:, g], ALU.add))
            for g in range(GROUPS):
                chain(dve.tensor_tensor(fw[:, g], Zh[:, g], Zh[:, g], ALU.mult))
            chain(dve.tensor_reduce(stat[:, 0, 0:8], num[:, 0:8, 0:MV], AX.X, ALU.add))
            dve.tensor_scalar(stat[:, 0, 0:8], stat[:, 0, 0:8], 1.0 / MV, EPS, ALU.mult, ALU.add).then_inc(h_var, 1)
            dve.wait_ge(h_root, 1)
            chain(dve.reciprocal(stat[:, 2, 0:8], stat[:, 1, 0:8]))
            dve.wait_ge(sig_o, 1)
            for g in range(GROUPS):
                Zf = Z[:, g, ZV:ZV + MH * MV]
                chain(dve.tensor_tensor(Zh[:, g], Zh[:, g], stat[:, 2, 4 * g:4 * g + 4].unsqueeze(2).to_broadcast([P, MH, MV]), ALU.mult))
                chain(dve.tensor_tensor(Zf, Zf, m_normw[:], ALU.mult))
                ins = dve.tensor_tensor(Zf, Zf, Zo[:, g], ALU.mult)
                chain(ins) if g == 0 else ins.then_inc(hm_ready, 1)

            HN = AH + AKV
            Zqk = Z[:, :, ZAQ:ZAV]
            chain(dve.tensor_scalar(qk_w[:, 0, :], qk_w[:, 0, :], HD ** -0.5, None, ALU.mult))
            dve.wait_ge(state_stored, 80)
            chain(dve.tensor_tensor(sq[:], Zqk, Zqk, ALU.mult))
            dve.wait_ge(hm_ready, 1)
            chain(dve.tensor_reduce(stat[:, 0, :], sq[:].rearrange("p g (h d) -> p (g h) d", d=HD), AX.X, ALU.add))
            dve.tensor_scalar(stat[:, 0, :], stat[:, 0, :], 1.0 / HD, EPS, ALU.mult, ALU.add).then_inc(qk_var, 1)
            dve.wait_ge(qk_root, 1)
            chain(dve.reciprocal(stat[:, 2, :], stat[:, 1, :]))
            for g in range(GROUPS):
                zg = Zqk[:, g].rearrange("p (h d) -> p h d", d=HD)
                chain(dve.tensor_tensor(zg, zg, stat[:, 2, HN * g:HN * (g + 1)].unsqueeze(2).to_broadcast([P, HN, HD]), ALU.mult))
                dve.tensor_tensor(zg[:, 0:AH], zg[:, 0:AH], qk_w[:, 0:1, :].to_broadcast([P, AH, HD]), ALU.mult).then_inc(dve_chain, 1)
                chain.n += 1
                ins = dve.tensor_tensor(zg[:, AH:HN], zg[:, AH:HN], qk_w[:, 1:2, :].to_broadcast([P, AKV, HD]), ALU.mult)
                ins.then_inc(k_normed, 1)
            dve.wait_ge(k_normed, 2)
            dve.wait_ge(dve_chain, chain.n)
            zl = Zqk[:, LAT].rearrange("p (h d) -> p h d", d=HD)
            t1 = sq[:, 0, :].rearrange("p (h d) -> p h d", d=HD)
            dve.tensor_tensor(t1, zl, cst[:, C_COS:C_COS + HD].unsqueeze(1).to_broadcast([P, HN, HD]), ALU.mult).then_inc(dve_chain, 1)
            chain.n += 1
            z4 = Zqk[:, LAT].rearrange("p (h a x f) -> p h a x f", a=2, x=2, f=HD // 4)
            t4 = sq[:, 1, :].rearrange("p (h a x f) -> p h a x f", a=2, x=2, f=HD // 4)
            s4 = cst[:, C_SIN:C_SIN + HD].rearrange("p (a x f) -> p a x f", a=2, x=2)
            for half in range(2):
                for xx in range(2):
                    sn = s4[:, half, xx, :].unsqueeze(1).to_broadcast([P, HN, HD // 4])
                    dve.tensor_tensor(t4[:, :, half, xx, :], z4[:, :, half, 1 - xx, :], sn, ALU.mult).then_inc(dve_chain, 1)
                    chain.n += 1
            dve.wait_ge(dve_chain, chain.n)
            dve.tensor_tensor(Zqk[:, LAT], sq[:, 0, :], sq[:, 1, :], ALU.add).then_inc(rope_done, 1)
            dve.wait_ge(rope_done, 1)
            for n, src in enumerate((Z[:, CTX, ZAK:ZAV], Z[:, LAT, ZAK:ZAV], cache_k[:])):
                dve.tensor_copy(k_dup[:, n, :, :, :], src.rearrange("p (k d) -> p k d", d=HD).unsqueeze(2).to_broadcast([P, AKV, 2, HD])
                                ).then_inc(k_dup_ready, 1)
            dve.wait_ge(kT_zeroed, 2)
            for n, (dst, o) in enumerate(((kTz_ctx, 0), (kTz_lat, 0), (kTz_lat, P))):
                dve.wait_ge(atT_ps, 5 + n)
                for a in range(2):
                    r = slice(64 * a, 64 * a + 64)
                    ins = dve.tensor_copy(dst[r, :, a, o:o + P], ps[r, n, :].rearrange("p (k s) -> p k s", k=AKV))
                ins.then_inc(kT_copied, 1)

            def maxima(i):
                heads = 4 if i < 4 else 2
                col = 4 * i if i < 4 else AH + 2 * (i - 4)
                mx = neg_max[:, col:col + heads]
                dve.wait_ge(score_ps, i + 1)
                chain(dve.tensor_reduce(mx, ps[:, i % 2, :].rearrange("p (h s) -> p h s", h=heads), AX.X, ALU.max))
                chain(dve.tensor_tensor(mx, mx, sink[:, col % AH:col % AH + heads], ALU.max))
                dve.tensor_scalar(mx, mx, -1.0, None, ALU.mult).then_inc(neg_max_ready, 1)

            def probT_copy(i):
                dve.wait_ge(probT_ps, i + 1)
                at_least(dve, pv_done, i - 1)
                dve.tensor_copy(probT[:, i % 2, :], ps[:, 2 + i % 2, :]).then_inc(probT_ready, 1)

            def normalised(g):
                dve.tensor_tensor(Z[:, g, ZAQ:ZAK].rearrange("p (h d) -> p h d", d=HD),
                                  ps[:, 4:6, :].rearrange("p a (h d) -> p (a h) d", d=HD),
                                  stat[:, 2, 0:AH].unsqueeze(2).to_broadcast([P, AH, HD]), ALU.mult).then_inc(ha_ready, 1)

            def sums(g):
                s = slice(AH * g, AH * (g + 1))
                dve.tensor_tensor(stat[:, 0, 0:AH], sink[:], neg_max[:, s], ALU.add).then_inc(sink_arg, 1)
                dve.wait_ge(sink_exp, g + 1)
                chain(dve.tensor_tensor(stat[:, 2, 0:AH], stat[:, 1, 0:AH], row_sum[:, s], ALU.add))
                chain(dve.reciprocal(stat[:, 2, 0:AH], stat[:, 2, 0:AH]))

            for i in range(13):
                if i < 12:
                    maxima(i)
                if i:
                    probT_copy(i - 1)
                if i == 5:
                    dve.wait_ge(neg_max_ready, 4)
                    sums(CTX)
                    dve.wait_ge(pv_done, 4)
                    normalised(CTX)
            dve.wait_ge(ha_ready, 1)
            sums(LAT)
            dve.wait_ge(pv_done, 12)
            normalised(LAT)

            def blocks_lo(lo, hi, hi_done, done):
                for j in range(8):
                    dve.wait_ge(hi_done, j + 1)
                    dve.tensor_tensor(lo[:, 2 * j:2 * j + 2, :].rearrange("p a t -> p (a t)"), ps[:, j, :],
                                      hi[:, 2 * j:2 * j + 2, :].bitcast(F32).rearrange("p a t -> p (a t)"),
                                      ALU.subtract).then_inc(done, 1)

            blocks_lo(hcT_lo, hcT_hi, hcT_hi_ready, hcT_lo_ready)
            dve.wait_ge(kv_stored, 32)

            def merge(n, ux):
                for k in range(24):
                    split(U_MERGE + k + AHEAD, ux)
                    if k == 19:
                        dve.wait_ge(units_done, U_MERGE + 20 + ux)
                        dve.wait_ge(sgm_ready, n + 1)
                        dve.tensor_tensor(sgm[:], sgm[:], ps[:, 4:6, :], ALU.mult).then_inc(gm_used, 1)
                    if k == 23:
                        dve.wait_ge(units_done, U_MERGE + 24 + ux)
                        dve.wait_ge(sga_ready, n + 1)
                        dve.tensor_tensor(sga[:], sga[:], ps[:, 6:8, :], ALU.mult).then_inc(ga_used, 1)
                        dve.wait_ge(ga_used, n + 1)
                        dve.tensor_tensor(mix[:, :, bass.ds(n * CH, CH)], sgm[:], sga[:], ALU.add).then_inc(mix_ready, 1)

            merge(0, 0)
            with dve.Fori(1, NCH) as n:
                merge(n, n * 24)
            blocks_lo(xT_lo, xT_hi, mixT_hi_ready, mixT_lo_ready)
            for n in range(NCH):
                for k in range(8):
                    split(U_OUT + 8 * n + k + AHEAD, 0)
                c = slice(n * CH, (n + 1) * CH)
                dve.wait_ge(units_done, U_OUT + 8 * n + 8)
                dve.wait_ge(gate_landed, 64)
                chain(dve.tensor_tensor(y_tmp[:], ps[:, 2 * (n % 2):2 * (n % 2) + 2, :], gate_bc[:, :, c], ALU.mult))
                dve.tensor_tensor(x[:, :, c], x[:, :, c], y_tmp[:], ALU.add).then_inc(x_updated, 1)
            scale(2, SC3)
            rms(2)
            norm(2, SH3)
            ffn(1, U_F2)


INPUTS = ["x_prompt", "x_sample", "cache_attn_k", "cache_attn_v", "state_mlstm_C", "state_mlstm_n", "state_mlstm_m",
          "c", "c_ctx", "ada_w", "ada_b", "norm_ffn1_w", "ffn1_wi", "ffn1_wo", "norm_mix_w", "w_in", "mlstm_gate_b",
          "mlstm_norm_w", "attn_q_norm_w", "attn_k_norm_w", "attn_sink", "w_proj_m", "w_proj_a", "w_out",
          "norm_ffn2_w", "ffn2_wi", "ffn2_wo"]
OUTPUTS = [("y_prompt", (1, P, D)), ("y_sample", (1, P, D)), ("new_attn_k", (1, 1, P, AKV, HD)),
           ("new_attn_v", (1, 1, P, AKV, HD)), ("new_mlstm_C", (1, 1, 2, MH, MV, MQK)),
           ("new_mlstm_n", (1, 1, 2, MH, MQK)), ("new_mlstm_m", (1, 1, 2, MH))]


def kernel(**inputs):
    import concourse.bacc as bacc
    from concourse.bass_utils import run_bass_kernel_spmd

    nc = bacc.Bacc("TRN2", target_bir_lowering=False, num_devices=1)
    arrays, I, O = {}, {}, {}
    for name in INPUTS + ["consts"]:
        a = np.ascontiguousarray(shape_constants() if name == "consts" else inputs[name])
        arrays[f"in_{name}"] = a
        I[name] = nc.dram_tensor(f"in_{name}", a.shape, F32, kind="ExternalInput").ap()
    for name, shape in OUTPUTS:
        O[name] = nc.dram_tensor(f"out_{name}", shape, F32, kind="ExternalOutput").ap()
    build(nc, I, O)
    r = run_bass_kernel_spmd(nc, [arrays], core_ids=[0])
    return tuple(r.results[0][f"out_{name}"] for name, _ in OUTPUTS)
```

```python
from contextlib import ExitStack

import numpy as np

import concourse.bass as bass
from concourse import mybir

F32 = mybir.dt.float32
F32R = mybir.dt.float32r
ALU = mybir.AluOpType
ACT = mybir.ActivationFunctionType
AX = mybir.AxisListType

P = 128
D = 2048
KD = D // P
GROUPS = 2
CTX, LAT = 0, 1
TOK = GROUPS * P
CH = 512
NCH = D // CH
D_FF = 5632
FCH = D_FF // CH
MH, MQK, MV = 4, 128, 256
AH, AKV, HD = 16, 4, 64
NMOD = 9
EPS = 1e-6
GRID_W = 64
NEG = -3.0e38

IN_GATES = 2 * MH * MQK + 2 * MH * MV
VW = MV + 1
ZQ, ZK, ZV = 0, MH * MQK, 2 * MH * MQK
ZO = ZV + MH * VW
ZAQ = ZO + MH * MV
ZAK = ZAQ + AH * HD
ZAV = ZAK + AKV * HD
ZW = ZAV + AKV * HD
ZCH = (ZW - MH) // CH
NG = 4 * MH
IN_GM = ZCH * CH + NG

U_F1 = 0
FFN_UNITS = 16 + (FCH - 1) * 24 + 8
U_IN = U_F1 + FFN_UNITS
U_MERGE = U_IN + 8 * ZCH
U_OUT = U_MERGE + 24 * NCH
U_F2 = U_OUT + 8 * NCH
U_END = U_F2 + FFN_UNITS
AHEAD = 3
RAW, SPL = 4, 4

SH1, SC1, G1, SH2, SC2, G2, SH3, SC3, G3 = range(NMOD)
ADA_PRE = 8

C_ID, C_TRI, C_MASK, C_COS, C_SIN, C_SEL, C_TWO = 0, 128, 384, 640, 704, 768, 800
C_W = 816


def shape_constants():
    c = np.zeros((P, C_W), np.float32)
    s, t = np.arange(P)[:, None], np.arange(P)[None, :]
    c[:, C_ID:C_ID + P] = s == t
    c[:, C_TRI:C_TRI + P] = s <= t
    c[:, C_TRI + P:C_TRI + 2 * P] = s >= t
    c[:, C_MASK:C_MASK + P] = np.where(s > t, 1e30, 0)
    c[:, C_MASK + P:C_MASK + 2 * P] = np.where(s < t, 1e30, 0)
    nf = HD // 4
    inv = np.float32(10000.0) ** (-np.arange(nf, dtype=np.float32) / np.float32(nf))
    for half, pos in enumerate((np.arange(P) // GRID_W, np.arange(P) % GRID_W)):
        ang = pos.astype(np.float32)[:, None] * inv
        o = half * 2 * nf
        c[:, C_COS + o:C_COS + o + nf] = c[:, C_COS + o + nf:C_COS + o + 2 * nf] = np.cos(ang)
        c[:, C_SIN + o:C_SIN + o + nf] = -np.sin(ang)
        c[:, C_SIN + o + nf:C_SIN + o + 2 * nf] = np.sin(ang)
    for j in range(4):
        c[32 * j, C_SEL] = c[32 * j + 1, C_SEL + 1] = 1
    for j in range(2 * NG):
        c[j, C_TWO + j % NG] = 1
    return c


class Chain:

    def __init__(self, eng, sem):
        self.eng, self.sem, self.n = eng, sem, 0

    def __call__(self, *instructions):
        for ins in instructions:
            self.n += 1
            ins.then_inc(self.sem, 1)
        self.eng.wait_ge(self.sem, self.n)


def build(nc, I, O):
    ctx = ExitStack()
    with ctx:
        def sem(name):
            return ctx.enter_context(nc.semaphore(name))

        def sems(name, n):
            return [sem(f"{name}{i}") for i in range(n)]

        BASE = (nc.sbuf_base + 63) // 64 * 64
        top = [BASE]

        def place(name, shape, dt=F32, at=None):
            if at is not None:
                top[0] = at
            size = 4 * int(np.prod(shape[1:]))
            t = nc.alloc_sbuf_tensor_at(name, shape, dt, offset=top[0])
            top[0] += (size + 31) // 32 * 32
            assert top[0] <= 229344, (name, top[0])
            return t

        x = place("x", [P, GROUPS, D])
        xT_hi = place("xT_hi", [P, KD, TOK], F32R)
        xT_lo = place("xT_lo", [P, KD, TOK], F32R)
        raw_w = place("raw_w", [P, RAW, 4, CH])
        w_hi = place("w_hi", [P, SPL, 2, CH], F32R)
        w_lo = place("w_lo", [P, SPL, 2, CH], F32R)
        cst = place("cst", [P, C_W])
        adacols = place("adacols", [P, NMOD * KD, GROUPS])
        ctile = place("ctile", [P, KD, 32])
        normw = place("normw", [P, 3, KD])
        acol = place("acol", [P, KD, GROUPS])
        small = place("small", [P, 64])
        gates = place("gates", [P, GROUPS, NG])
        ROWS = top[0]
        colrows = place("colrows", [80, P])
        diag = place("diag", [P, GROUPS, P], at=ROWS)
        gate_rows = place("gate_rows", [2 * KD, 2, P], at=ROWS)
        SLOT = top[0]
        acc = place("acc", [P, GROUPS, D])
        AFTER_ACC = top[0]
        h = place("h", [P, GROUPS, CH])
        sg = place("sg", [P, GROUPS, CH])
        hT_hi = place("hT_hi", [P, 4, TOK], F32R)
        hT_lo = place("hT_lo", [P, 4, TOK], F32R)
        xm = place("xm", [P, KD, TOK], at=AFTER_ACC)
        Z = place("Z", [P, GROUPS, ZW], at=SLOT)
        SCR = top[0]
        ada_w_sb = place("ada_w_sb", [P, 4, 4, CH])
        AFTER_ADA = top[0]
        gate_bc = place("gate_bc", [P, GROUPS, D], at=SCR + 16384)
        y_tmp = place("y_tmp", [P, GROUPS, CH], at=SCR)
        top[0] = AFTER_ADA
        ada_bias = place("ada_bias", [P, 2, CH])
        ada_rows_sb = place("ada_rows_sb", [P, CH])
        AFTER_ROWS = top[0]
        wg_raw = place("wg_raw", [P, KD, NG])
        wg = place("wg", [P, KD, 2, NG], F32R)
        AFTER_WG = top[0]
        gT = place("gT", [2 * NG, TOK], at=AFTER_ROWS)
        top[0] = AFTER_WG
        gateb = place("gateb", [P, NG])
        END = top[0]
        cache_k = place("cache_k", [P, AKV * HD])
        cache_v = place("cache_v", [P, AKV * HD])
        MN = top[0]
        m_normw = place("m_normw", [P, MH * MV])
        head_tmp = place("head_tmp", [P, AH, HD], at=MN)
        qk_w = place("qk_w", [P, 2, HD])
        sink = place("sink", [P, AH])
        m0_bc = place("m0_bc", [P, 2, MH])
        m0_row = place("m0_row", [40, 1])
        NC = 2 * GROUPS * MH
        absf = place("absf", [P, NC])
        lf = place("lf", [P, 2, GROUPS * MH])
        bcol = place("bcol", [P, 2, GROUPS * MH])
        apad = place("apad", [P, 2, 32])
        mcol = place("mcol", [P, 2, GROUPS * MH])
        mt = place("mt", [P, 2, GROUPS * MH])
        exp_negm = place("exp_negm", [P, NC])
        decay = place("decay", [P, 2, MH])
        wk = place("wk", [P, MH, 2])
        den = place("den", [P, NC])
        scan = [place(f"scan{i}", [40, 2 * P]) for i in range(2)]
        n0_rows = place("n0_rows", [2 * MH, P])
        stat = place("stat", [P, 3, 2 * (AH + AKV)])
        row_sum = place("row_sum", [P, 2 * AH])
        NM = top[0]
        neg_max = place("neg_max", [P, 2 * AH])
        hstat = place("hstat", [P, 4, GROUPS * MH], at=NM)
        num = place("num", [P, NC, MV + 1], at=SCR)
        c_raw = place("c_raw", [P, 2 * MH * 2, MQK], at=SCR)
        CT = place("CT", [P, 2 * MH, MV + 1], at=SCR + 16480)
        c_new = place("c_new", [P, 2, MH * 2, MQK], at=SCR + 16480)
        qkT = place("qkT", [P, 4, MH, P], at=SCR + 16480 + 8256)
        decays = place("decays", [P, 2, MH, P])
        sT = place("sT", [P, 2, MH, P])
        v_wk = place("v_wk", [P, 2, MH, MV], at=SCR + 16480 + 16448)
        assert top[0] <= END
        k_dup = place("k_dup", [P, 3, AKV, 2, HD], at=SCR)
        kTz_ctx = place("kTz_ctx", [P, AKV, 2, P])
        prob = place("prob", [P, 2, CH])
        kTz_lat = place("kTz_lat", [P, AKV, 2, 2 * P], at=SCR + 16480)
        qT = place("qT", [P, GROUPS, AH // 2, P], at=SCR + 16480 + 8256 + 2048)
        probT = place("probT", [P, 2, CH])
        assert top[0] <= END
        hcT_hi = place("hcT_hi", [P, KD, TOK], F32R, at=SCR)
        hcT_lo = place("hcT_lo", [P, KD, TOK], F32R)
        sgm = place("sgm", [P, GROUPS, CH], at=SLOT)
        sga = place("sga", [P, GROUPS, CH])
        mix = place("mix", [P, GROUPS, D], at=SLOT + 16384)
        n_new = place("n_new", [2, MH * P], at=SCR + 16480 + 8256)
        ps = nc.alloc_psum_tensor("ps", [P, 8, CH], F32)

        gate_dram = nc.dram_tensor("gate_dram", (3, KD, GROUPS, P), F32).ap()
        ident = cst[:, C_ID:C_ID + P]

        raw_landed = sems("raw_landed", RAW)
        hi_ready, lo_ready, units_done = sem("hi_ready"), sem("lo_ready"), sem("units_done")
        cst_landed, rows_landed, x_landed = sem("cst_landed"), sem("rows_landed"), sem("x_landed")
        cols_ps, cond_silu, zeroed = sem("cols_ps"), sem("cond_silu"), sem("zeroed")
        ada_landed, bias_landed = sems("ada_landed", 4), sems("bias_landed", 2)
        ada_used, ada_rows_done = sem("ada_used"), sem("ada_rows_done")
        ada_sel_done, ada_cols_done = sem("ada_sel_done"), sem("ada_cols_done")
        sumsq_ready, var_ready, root_ready, diag_ready = sem("sumsq_ready"), sem("var_ready"), sem("root_ready"), sem("diag_ready")
        gT_ps, gT_ready, ada_blk_ready, ada_T_done = sem("gT_ps"), sem("gT_ready"), sem("ada_blk_ready"), sem("ada_T_done")
        bias_zeroed, xm_act, acol_ready = sem("bias_zeroed"), sem("xm_act"), sem("acol_ready")
        gate_rows_ps, gate_rows_ready, gate_stored, gate_landed = (
            sem("gate_rows_ps"), sem("gate_rows_ready"), sem("gate_stored"), sem("gate_landed"))
        norm_ps, xm_ready, xT_hi_ready, xT_lo_ready = sem("norm_ps"), sem("xm_ready"), sem("xT_hi_ready"), sem("xT_lo_ready")
        silu_done, h_done, hT_ps, hT_hi_ready, hT_lo_ready, acc_done = (
            sem("silu_done"), sem("h_done"), sem("hT_ps"), sem("hT_hi_ready"), sem("hT_lo_ready"), sem("acc_done"))
        x_updated = sem("x_updated")
        dve_chain, act_chain = sem("dve_chain"), sem("act_chain")
        out_landed = sem("out_landed")
        wg_landed, wg_hi_ready, wg_ready, gates_ps = (
            sem("wg_landed"), sem("wg_hi_ready"), sem("wg_ready"), sem("gates_ps"))
        z_copied, misc_landed = sem("z_copied"), sem("misc_landed")
        absf_ready, softplus_ready, lf_ready, b_ps, a_ready, aT_ps, scan_done, mT_ps = (
            sem("absf_ready"), sem("softplus_ready"), sem("lf_ready"), sem("b_ps"), sem("a_ready"),
            sem("aT_ps"), sem("scan_done"), sem("mT_ps"))
        m_ready, m_last_ps, wk_arg, wk_ready, mt_ready, exps_ready = (
            sem("m_ready"), sem("m_last_ps"), sem("wk_arg"), sem("wk_ready"), sem("mt_ready"), sem("exps_ready"))
        c_landed, qkT_ps, qkT_copied, CT_ps, CT_copied = (
            sem("c_landed"), sem("qkT_ps"), sem("qkT_copied"), sem("CT_ps"), sem("CT_copied"))
        qkT_copied_act, CT_copied_act = sem("qkT_copied_act"), sem("CT_copied_act")
        qk_ps, mb_ps, decays_ready, sT_ready, sv_ps, sv_copied, inter_ps, inter_added = (
            sem("qk_ps"), sem("mb_ps"), sem("decays_ready"), sem("sT_ready"), sem("sv_ps"), sem("sv_copied"),
            sem("inter_ps"), sem("inter_added"))
        v_wk_ready, state_ps, state_copied, state_copied_act = (
            sem("v_wk_ready"), sem("state_ps"), sem("state_copied"), sem("state_copied_act"))
        h_var, h_root, hm_ready = sem("h_var"), sem("h_root"), sem("hm_ready")
        ones_ready, zo_ready, qk_rinv, pool_chain, den_ready, fw_ready, h_summed, h_squared = (
            sem("ones_ready"), sem("zo_ready"), sem("qk_rinv"), sem("pool_chain"), sem("den_ready"), sem("fw_ready"),
            sem("h_summed"), sem("h_squared"))
        kT_zeroed, qk_var, qk_root, rope_done, k_dup_ready = (
            sem("kT_zeroed"), sem("qk_var"), sem("qk_root"), sem("rope_done"), sem("k_dup_ready"))
        atT_ps, qT_copied, kT_copied = sem("atT_ps"), sem("qT_copied"), sem("kT_copied")
        score_ps, neg_max_ready, prob_ready, probT_ps, probT_ready, pv_done, sink_exp, ha_ready = (
            sem("score_ps"), sem("neg_max_ready"), sem("prob_ready"), sem("probT_ps"), sem("probT_ready"),
            sem("pv_done"), sem("sink_exp"), sem("ha_ready"))
        hcT_ps, hcT_hi_ready, hcT_lo_ready = sem("hcT_ps"), sem("hcT_hi_ready"), sem("hcT_lo_ready")
        sgm_ready, sga_ready, gm_used, ga_used, mix_ready = (
            sem("sgm_ready"), sem("sga_ready"), sem("gm_used"), sem("ga_used"), sem("mix_ready"))
        mixT_ps, mixT_hi_ready, mixT_lo_ready = sem("mixT_ps"), sem("mixT_hi_ready"), sem("mixT_lo_ready")
        state_stored, kv_stored, sink_arg = sem("state_stored"), sem("kv_stored"), sem("sink_arg")

        def at_least(eng, s, v):
            if not isinstance(v, int) or v > 0:
                eng.wait_ge(s, v)

        blk = ctx.enter_context(nc.Block())

        @blk.sync
        def _(sp):
            sp.dma_start(cst[:], I["consts"]).then_inc(cst_landed, 16)
            for n, name in enumerate(("c_ctx", "c", "norm_ffn1_w", "norm_mix_w", "norm_ffn2_w")):
                src = I[name].rearrange("(k p) -> k p", p=P) if len(I[name].shape) == 1 else \
                    I[name].rearrange("a (k p) -> (a k) p", p=P)
                sp.dma_start(colrows[16 * n:16 * n + 16, :], src).then_inc(rows_landed, 16)
            sp.wait_ge(ada_used, 8)
            sp.dma_start(x[:, CTX, :], I["x_prompt"][0]).then_inc(x_landed, 16)
            sp.dma_start(x[:, LAT, :], I["x_sample"][0]).then_inc(x_landed, 16)
            sp.wait_ge(ada_used, 4 * ADA_PRE - 4)

            def tile(ts, tx, src):
                at_least(sp, lo_ready, 2 * (ts + tx) - 2 * RAW + 2)
                sp.dma_start(raw_w[:, ts % RAW, :, :], src).then_inc(raw_landed[ts % RAW], 16)

            def rows(w, q):
                return w[0].rearrange("(q k p) n -> q p k n", k=4, p=P)[q]

            def ffn(f, t0):
                wi, wo = I[f"ffn{f + 1}_wi"], I[f"ffn{f + 1}_wo"]

                def ffn_in(i, ts, tx):
                    for part in range(2):
                        for q in range(4):
                            tile(ts + 4 * part + q, tx, rows(wi, q)[:, :, bass.ds(i * CH + part * D_FF, CH)])

                def ffn_out(j, ts, tx):
                    src = wo[0].rearrange("(q k p) n -> p q k n", k=4, p=P)
                    for n in range(NCH):
                        s = src[:, bass.ds(j, 1), :, n * CH:(n + 1) * CH]
                        tile(ts + n, tx, s.rearrange("p a k n -> p (a k) n"))

                ffn_in(0, t0, 0)
                with sp.Fori(1, FCH) as i:
                    ffn_in(i, t0 + 8, (i - 1) * 12)
                    ffn_out(i - 1, t0 + 16, (i - 1) * 12)
                ffn_out(FCH - 1, t0 + 8 + 12 * (FCH - 1), 0)

            ffn(0, U_F1 // 2)
            w_in = I["w_in"]
            with sp.Fori(0, 3) as i:
                for c in range(2):
                    for q in range(4):
                        tile(U_IN // 2 + 4 * c + q, i * 8, rows(w_in, q)[:, :, bass.ds(i * (2 * CH) + c * CH, CH)])
            for c in range(6, ZCH):
                for q in range(4):
                    tile(U_IN // 2 + 4 * c + q, 0, rows(w_in, q)[:, :, c * CH + NG:(c + 1) * CH + NG])
            with sp.Fori(0, NCH) as n:
                for q in range(4):
                    tile(U_MERGE // 2 + q, n * 12, rows(w_in, q)[:, :, bass.ds(n * CH + IN_GM, CH)])
                for q in range(4):
                    tile(U_MERGE // 2 + 4 + q, n * 12, rows(w_in, q)[:, :, bass.ds(n * CH + IN_GM + D, CH)])
                for q in range(2):
                    tile(U_MERGE // 2 + 8 + q, n * 12, rows(I["w_proj_m"], q)[:, :, bass.ds((n + n) * (CH // 2), CH)])
                for q in range(2):
                    tile(U_MERGE // 2 + 10 + q, n * 12, rows(I["w_proj_a"], q)[:, :, bass.ds((n + n) * (CH // 2), CH)])
            with sp.Fori(0, NCH) as n:
                for q in range(4):
                    tile(U_OUT // 2 + q, n * 4, rows(I["w_out"], q)[:, :, bass.ds(n * CH, CH)])
            ffn(1, U_F2 // 2)
            for n in range(NCH):
                sp.wait_ge(x_updated, 2 * NCH + n + 1)
                for g, name in enumerate(("y_prompt", "y_sample")):
                    sp.dma_start(O[name][0][:, n * CH:(n + 1) * CH], x[:, g, n * CH:(n + 1) * CH]).then_inc(out_landed, 16)
            sp.wait_ge(out_landed, 16 * 2 * NCH)
            sp.wait_ge(state_stored, 16 * 5)
            sp.wait_ge(kv_stored, 16 * 2)

        @blk.gpsimd
        def _(pool):
            pool.memset(acc[:], 0.0).then_inc(acc_done, 1)
            pool.wait_ge(ada_used, 4 * ADA_PRE + 4)
            def all_rows(ap, n):
                return ap.broadcast_to([P, n])

            pool.dma_start(wg_raw[:], I["w_in"][0].rearrange("(k p) n -> p k n", p=P)[:, :, IN_GATES:IN_GATES + NG]).then_inc(wg_landed, 16)
            for dst, src in (
                    (gateb[:], all_rows(I["mlstm_gate_b"], NG)),
                    (cache_k[:], I["cache_attn_k"][0, 0].rearrange("s k d -> s (k d)")),
                    (cache_v[:], I["cache_attn_v"][0, 0].rearrange("s k d -> s (k d)")),
                    (m_normw[:], all_rows(I["mlstm_norm_w"], MH * MV)),
                    (qk_w[:, 0, :], all_rows(I["attn_q_norm_w"], HD)),
                    (qk_w[:, 1, :], all_rows(I["attn_k_norm_w"], HD)),
                    (sink[:], all_rows(I["attn_sink"], AH)),
                    (m0_bc[:].rearrange("p d h -> p (d h)"),
                     all_rows(I["state_mlstm_m"][0].rearrange("a d h -> a (d h)"), 2 * MH)),
                    (n0_rows[:], I["state_mlstm_n"][0, 0].rearrange("d h k -> (d h) k"))):
                pool.dma_start(dst, src).then_inc(misc_landed, 16)
            pool.wait_ge(zeroed, 1)
            for d in range(2):
                pool.dma_start(m0_row[32 * d + MH:32 * d + 2 * MH, :],
                             I["state_mlstm_m"][0, 0, d].rearrange("(h a) -> h a", a=1)).then_inc(misc_landed, 16)


            def gate_load(r):
                for g in range(GROUPS):
                    row = gate_dram[r].rearrange("(a k) g p -> g a k p", a=1)[g]
                    pool.dma_start(gate_bc[:, g, :].rearrange("q (k p) -> q k p", p=P),
                                   row.broadcast_to([P, KD, P])).then_inc(gate_landed, 16)

            def gate_store(r, at):
                pool.dma_start(gate_dram[r].rearrange("k g p -> (k g) p"), gate_rows[:, at, :]).then_inc(gate_stored, 16)

            pool.wait_ge(gate_rows_ready, FCH - 1)
            gate_store(0, 0)
            pool.wait_ge(gate_stored, 16)
            pool.wait_ge(ada_used, 4 * (ADA_PRE + 2 * (FCH - 1)))
            gate_load(0)
            pool.wait_ge(z_copied, 6)
            for g in range(GROUPS):
                zo = Z[:, g, ZO:ZO + MH * MV]
                ins = pool.tensor_tensor(zo, zo, m_normw[:], ALU.mult)
            ins.then_inc(zo_ready, 1)
            pool.wait_ge(gate_rows_ready, FCH)
            gate_store(1, 0)
            gate_store(2, 1)
            pool.wait_ge(ada_used, NMOD * KD)
            pool.dma_start(c_raw[:], I["state_mlstm_C"][0, 0].rearrange("d h (a p) k -> p (d h a) k", p=P)).then_inc(c_landed, 16)
            chain = Chain(pool, pool_chain)
            HN = AH + AKV
            pool.wait_ge(qk_rinv, 1)
            for g in range(GROUPS):
                z = Z[:, g, ZAQ:ZAV].rearrange("p (h d) -> p h d", d=HD)
                chain(pool.tensor_tensor(z, z, stat[:, 2, HN * g:HN * (g + 1)].unsqueeze(2).to_broadcast([P, HN, HD]), ALU.mult))
                for n, (h0, h1) in enumerate(((0, AH), (AH, HN))):
                    ins = pool.tensor_tensor(z[:, h0:h1], z[:, h0:h1], qk_w[:, n:n + 1, :].to_broadcast([P, h1 - h0, HD]), ALU.mult)
                    chain(ins)
            pool.dma_start(O["new_attn_k"][0, 0].rearrange("s k d -> s (k d)"), Z[:, CTX, ZAK:ZAV]).then_inc(kv_stored, 16)
            pool.dma_start(O["new_attn_v"][0, 0].rearrange("s k d -> s (k d)"), Z[:, CTX, ZAV:ZW]).then_inc(kv_stored, 16)
            sin = cst[:, C_SIN:C_SIN + HD].rearrange("p (a x f) -> p a x f", a=2, x=2)
            for h0, h1 in ((0, AH), (AH, HN)):
                n = h1 - h0
                z = Z[:, LAT, ZAQ + h0 * HD:ZAQ + h1 * HD].rearrange("p (h d) -> p h d", d=HD)
                z4, t4 = (t.rearrange("p h (a x f) -> p h a x f", a=2, x=2) for t in (z, head_tmp[:, 0:n, :]))
                for half in range(2):
                    for xx in range(2):
                        chain(pool.tensor_tensor(t4[:, :, half, xx, :], z4[:, :, half, 1 - xx, :],
                                                 sin[:, half, xx, :].unsqueeze(1).to_broadcast([P, n, HD // 4]), ALU.mult))
                chain(pool.tensor_tensor(z, z, cst[:, C_COS:C_COS + HD].unsqueeze(1).to_broadcast([P, n, HD]), ALU.mult))
                ins = pool.tensor_tensor(z, z, head_tmp[:, 0:n, :], ALU.add)
                if h0 == 0:
                    chain(ins)
            ins.then_inc(rope_done, 1)
            pool.wait_ge(mt_ready, 1)
            pool.dma_start(O["new_mlstm_m"][0, 0:1, 0, :], mt[P - 1:P, 0, 0:MH]).then_inc(state_stored, 16)
            pool.dma_start(O["new_mlstm_m"][0, 0:1, 1, :], mt[0:1, 1, 0:MH]).then_inc(state_stored, 16)
            pool.wait_ge(state_copied, 3)
            pool.wait_ge(state_copied_act, 2)
            for d in range(2):
                pool.dma_start(O["new_mlstm_C"][0, 0, d].rearrange("h (a p) k -> p (h a) k", p=P),
                               c_new[:, d, :, :]).then_inc(state_stored, 16)
            pool.dma_start(O["new_mlstm_n"][0, 0].rearrange("d h k -> d (h k)"), n_new[:]).then_inc(state_stored, 16)
            pool.wait_ge(h_squared, GROUPS * MH)
            pool.memset(kTz_ctx[:], 0.0).then_inc(kT_zeroed, 1)
            pool.wait_ge(state_stored, 80)
            pool.memset(kTz_lat[:], 0.0).then_inc(kT_zeroed, 1)
            pool.wait_ge(mix_ready, NCH)
            pool.memset(acc[:], 0.0).then_inc(acc_done, 1)
            pool.wait_ge(units_done, U_OUT)
            pool.wait_ge(gate_stored, 48)
            gate_load(1)
            pool.wait_ge(x_updated, 2 * NCH)
            gate_load(2)

        @blk.tensor
        def _(pe):
            def ada_acc(c):
                at_least(pe, ada_rows_done, c)
                for q in range(4):
                    pe.wait_ge(ada_landed[q], 16 * (c + 1))
                    for j in range(4):
                        mm = pe.matmul(ps[32 * j:32 * j + 32, 6, :], ctile[:, 4 * q + j, :],
                                       ada_w_sb[:, q, j, :], start=(q == 0), stop=(q == 3))
                    mm.then_inc(ada_used, 1)
                    last = mm

            def ada_sel(c):
                pe.wait_ge(ada_rows_done, c + 1)
                at_least(pe, ada_cols_done, c)
                for b in range(4):
                    mm = pe.matmul(ps[32 * b:32 * b + 32, 7, 0:P], cst[:, C_SEL:C_SEL + 32],
                                   ada_rows_sb[:, b * P:(b + 1) * P], start=True, stop=True)
                mm.then_inc(ada_sel_done, 1)

            def ada_T(c):
                pe.wait_ge(ada_blk_ready, c + 1)
                pe.transpose(ps[:, 7, P:2 * P], ada_rows_sb[:, 0:P], ident).then_inc(ada_T_done, 1)

            def norm(s, banks=range(8)):
                pe.wait_ge(diag_ready, s + 1)
                for j in banks:
                    for b in range(2):
                        for g in range(GROUPS):
                            k = 2 * j + b
                            mm = pe.matmul(ps[:, j, b * TOK + g * P:b * TOK + (g + 1) * P],
                                           x[:, g, k * P:(k + 1) * P], diag[:, g, :], start=True, stop=True)
                    mm.then_inc(norm_ps, 1)

            def unit(us, ux, hi, lo, kb, banks, first, last):
                pe.wait_ge(lo_ready, us + ux + 1)
                slot = us % SPL
                for kk in range(2):
                    for g in range(GROUPS):
                        a_hi = hi[:, kb + kk, g * P:(g + 1) * P]
                        a_lo = lo[:, kb + kk, g * P:(g + 1) * P]
                        out = ps[:, banks + g, :]
                        pe.matmul(out, a_hi, w_hi[:, slot, kk, :], start=(first and kk == 0), stop=False)
                        pe.matmul(out, a_hi, w_lo[:, slot, kk, :], start=False, stop=False)
                        mm = pe.matmul(out, a_lo, w_hi[:, slot, kk, :], start=False, stop=(last and kk == 1))
                mm.then_inc(units_done, 1)

            def x_chunk(us, ux, banks, between=None, stage=None):
                for k in range(8):
                    if stage is not None:
                        pe.wait_ge(xT_lo_ready, 8 * stage + max(k + 1, 2))
                    unit(us + k, ux, xT_hi, xT_lo, 2 * k, banks, k == 0, k == 7)
                    if between:
                        between(k)

            def gate_T(vecs):
                for n, vec in enumerate(vecs):
                    mm = pe.transpose(ps[0:2 * KD, 7, n * P:(n + 1) * P],
                                      adacols[:, vec * KD:(vec + 1) * KD, :].rearrange("p k g -> p (k g)"), ident)
                mm.then_inc(gate_rows_ps, 1)

            def ffn(f, u0, stage):
                def ffn_in(i, us, ux, ada=None):
                    def g_between(k):
                        if ada is not None:
                            if k == 0:
                                ada_acc(ada)
                            if k == 2:
                                ada_sel(ada)
                            if k == 4:
                                ada_T(ada)
                            if k == 6:
                                pe.wait_ge(ada_cols_done, ada + 1)
                                gate_T((G1,))

                    def u_between(k):
                        if ada is not None:
                            if k == 4:
                                ada_acc(ada + 1)
                            if k == 6:
                                pe.wait_ge(gate_rows_ready, i)
                                ada_sel(ada + 1)
                            if k == 7:
                                ada_T(ada + 1)

                    first = isinstance(i, int)
                    if not first:
                        pe.wait_ge(silu_done, FCH * f + i)
                    x_chunk(us, ux, 0, g_between, stage if first else None)
                    if not first:
                        pe.wait_ge(h_done, FCH * f + i)
                        pe.wait_ge(acc_done, 45 * f + 4 * i - 3)
                    x_chunk(us + 8, ux, 2, u_between)

                def ffn_out(j, us, ux, epilogue=False):
                    for n in range(NCH):
                        banks = 4 if n % 2 == 0 else 2
                        if n == 0:
                            pe.wait_ge(hT_lo_ready, FCH * f + j + 1)
                        elif n == 1:
                            if epilogue:
                                pe.wait_ge(acc_done, 45 * f + 4 * j + 1)
                            else:
                                pe.wait_ge(h_done, FCH * f + j + 2)
                        else:
                            pe.wait_ge(acc_done, 45 * f + 4 * j + n)
                        for k in range(2):
                            unit(us + 2 * n + k, ux, hT_hi, hT_lo, 2 * k, banks, k == 0, k == 1)

                def h_transposes(i):
                    pe.wait_ge(h_done, FCH * f + i + 1)
                    if not isinstance(i, int):
                        pe.wait_ge(acc_done, 45 * f + 4 * i)
                    for b in range(4):
                        for g in range(GROUPS):
                            mm = pe.transpose(ps[:, 4 + b // 2, (b % 2) * TOK + g * P:(b % 2) * TOK + (g + 1) * P],
                                              h[:, g, b * P:(b + 1) * P], ident)
                    mm.then_inc(hT_ps, 1)

                ffn_in(0, u0, 0)
                h_transposes(0)
                with pe.Fori(1, FCH) as i:
                    ffn_in(i, u0 + 16, (i - 1) * 24, 2 * i + ADA_PRE - 2 if f == 0 else None)
                    ffn_out(i - 1, u0 + 32, (i - 1) * 24)
                    h_transposes(i)
                ffn_out(FCH - 1, u0 + 16 + 24 * (FCH - 1), 0, True)

            pe.wait_ge(cst_landed, 16)
            pe.wait_ge(rows_landed, 80)
            pe.transpose(ps[:, 0, 0:80], colrows[:, :], cst[0:80, C_ID:C_ID + 80]).then_inc(cols_ps, 1)
            pe.wait_ge(cond_silu, 1)
            for c in range(ADA_PRE):
                ada_acc(c)
                ada_sel(c)
                ada_T(c)
                if c == 5:
                    norm(0, range(6))
            pe.wait_ge(ada_cols_done, ADA_PRE)
            norm(0, range(6, 8))
            ffn(0, U_F1, 0)

            norm(1)
            def z_pair(c, ux):
                for m in range(2):
                    at_least(pe, z_copied, c + m - 1)

                    def between(k):
                        if k == 3:
                            ada_acc(c + m + 4 * G2 + 8)
                        if k == 5:
                            ada_sel(c + m + 4 * G2 + 8)
                        if k == 6:
                            ada_T(c + m + 4 * G2 + 8)

                    x_chunk(U_IN + 8 * m, ux, 2 * m, between, 1 if isinstance(c, int) and m == 0 else None)

            z_pair(0, 0)
            pe.wait_ge(wg_ready, 1)
            for k in range(KD):
                for half, xT in enumerate((xT_hi, xT_lo)):
                    mm = pe.matmul(ps[0:2 * NG, 4, 0:TOK], wg[:, k, :, :].rearrange("p a n -> p (a n)"), xT[:, k, :],
                                   start=(k + half == 0), stop=(k == KD - 1 and half == 1))
            mm.then_inc(gT_ps, 1)
            pe.wait_ge(gT_ready, 1)
            for g in range(GROUPS):
                mm = pe.matmul(ps[:, 5, g * NG:(g + 1) * NG], gT[:, g * P:(g + 1) * P], cst[0:2 * NG, C_TWO:C_TWO + NG],
                               start=True, stop=True)
            mm.then_inc(gates_ps, 1)
            with pe.Fori(1, 4) as i:
                z_pair(2 * i, i * 16)
            pe.wait_ge(ada_cols_done, NMOD * 4)
            gate_T((G2, G3))
            pe.wait_ge(z_copied, 7)
            x_chunk(U_IN + 64, 0, 0)

            def gm_unit(k):
                unit(U_MERGE + k, 0, xT_hi, xT_lo, 2 * k, 6, k == 0, k == 7)

            pe.wait_ge(gate_rows_ready, FCH)
            for k in range(2):
                gm_unit(k)
            pe.wait_ge(lf_ready, 1)
            for d in range(2):
                mm = pe.matmul(ps[:, 4, 8 * d:8 * d + 8], cst[:, C_TRI + d * P:C_TRI + (d + 1) * P], lf[:, d, :],
                               start=True, stop=True)
            mm.then_inc(b_ps, 1)
            pe.wait_ge(a_ready, 1)
            pe.transpose(ps[0:40, 5, 0:P], apad[:].rearrange("p d c -> p (d c)")[:, 0:40], ident).then_inc(aT_ps, 1)
            pe.wait_ge(z_copied, ZCH)
            for n in range(4):
                for hd in range(MH):
                    o = (ZQ, ZK)[n // 2] + hd * MQK
                    mm = pe.transpose(ps[:, n, hd * P:(hd + 1) * P], Z[:, n % 2, o:o + MQK], ident)
                mm.then_inc(qkT_ps, 1)
            for k in range(2, AHEAD):
                gm_unit(k)
            pe.wait_ge(scan_done, 14)
            pe.transpose(ps[:, 4, 0:40], scan[1][:, P // 2:P // 2 + P], cst[0:40, C_ID:C_ID + 40])
            pe.wait_ge(misc_landed, 16 * 11)
            pe.transpose(ps[:, 4, 40:40 + 2 * MH], n0_rows[:], cst[0:2 * MH, C_ID:C_ID + 2 * MH]).then_inc(mT_ps, 1)
            pe.wait_ge(m_ready, 1)
            for d in range(2):
                last = (P - 1, 0)[d]
                mm = pe.matmul(ps[:, 5, 4 * d:4 * d + 4], cst[:, C_ID + last:C_ID + last + 1].to_broadcast([P, P]),
                               mcol[:, d, 0:MH], start=True, stop=True)
            mm.then_inc(m_last_ps, 1)
            pe.wait_ge(wk_arg, 2)
            pe.wait_ge(qkT_copied, 2)
            pe.wait_ge(qkT_copied_act, 2)
            pe.wait_ge(c_landed, 16)
            for n in range(4):
                for j in range(4):
                    mm = pe.transpose(ps[:, 2 + n, j * P:(j + 1) * P], c_raw[:, 4 * n + j, :], ident)
                mm.then_inc(CT_ps, 1)
            for g in range(GROUPS):
                for hd in range(MH):
                    mm = pe.matmul(ps[:, g, hd * P:(hd + 1) * P], qkT[:, 2 + g, hd, :], qkT[:, g, hd, :],
                                   start=True, stop=True)
                mm.then_inc(qk_ps, 1)
            pe.wait_ge(CT_copied, 3)
            pe.wait_ge(CT_copied_act, 2)

            def m_rows(i):
                d, g = i // 2, i % 2
                at_least(pe, decays_ready, i - 1)
                for hd in range(MH):
                    out = ps[:, 2 + i % 2, hd * P:(hd + 1) * P]
                    pe.matmul(out, ident, cst[:, C_MASK + d * P:C_MASK + (d + 1) * P], start=True, stop=False)
                    mm = pe.matmul(out, mcol[:, d, g * MH + hd:g * MH + hd + 1].to_broadcast([P, P]), ident,
                                   start=False, stop=True)
                mm.then_inc(mb_ps, 1)

            def sv(i):
                d, g = i // 2, i % 2
                pe.wait_ge(sT_ready, i + 1)
                for hd in range(MH):
                    n = 4 * i + hd
                    at_least(pe, sv_copied, n - 1)
                    pe.matmul(ps[:, 4 + n % 2, 0:VW], sT[:, i % 2, hd, :], Z[:, g, ZV + hd * VW:ZV + (hd + 1) * VW],
                              start=True, stop=True).then_inc(sv_ps, 1)

            pe.wait_ge(ones_ready, 1)
            for i in range(5):
                if i < 4:
                    m_rows(i)
                if i:
                    sv(i - 1)
            for n in range(2 * MH):
                d, hd = n // MH, n % MH
                at_least(pe, inter_added, n - 1)
                pe.matmul(ps[:, 2 + n % 2, 0:MV + 1], qkT[:, LAT, hd, :], CT[:, n, :], start=True, stop=True).then_inc(inter_ps, 1)
            pe.wait_ge(v_wk_ready, 2)
            pe.wait_ge(sv_copied, 16)
            for n in range(4):
                for j in range(4):
                    d, hd, a = n // 2, 2 * (n % 2) + j // 2, j % 2
                    mm = pe.matmul(ps[:, 2 + n, j * P:(j + 1) * P], v_wk[:, d, hd, a * P:(a + 1) * P],
                                   Z[:, CTX, ZK + hd * MQK:ZK + (hd + 1) * MQK], start=True, stop=True)
                mm.then_inc(state_ps, 1)
            for hd in range(MH):
                mm = pe.matmul(ps[0:2, 0, hd * P:(hd + 1) * P], wk[:, hd, :], Z[:, CTX, ZK + hd * MQK:ZK + (hd + 1) * MQK],
                               start=True, stop=True)
            mm.then_inc(state_ps, 1)

            pe.wait_ge(rope_done, 1)
            pe.wait_ge(state_copied, 3)
            pe.wait_ge(state_copied_act, 2)
            for n in range(4):
                g = n // 2
                for j in range(4):
                    o = ZAQ + (4 * (n % 2) + j) * P
                    mm = pe.transpose(ps[:, n, j * P:(j + 1) * P], Z[:, g, o:o + P], ident)
                mm.then_inc(atT_ps, 1)
            for k in range(AHEAD, 2 * AHEAD - 1):
                gm_unit(k)
            pe.wait_ge(k_dup_ready, 3)
            for n in range(3):
                pe.wait_ge(qT_copied, n + 1)
                for kv in range(AKV):
                    mm = pe.transpose(ps[:, n, kv * P:(kv + 1) * P], k_dup[:, n, kv, :, :].rearrange("p a d -> p (a d)"), ident)
                mm.then_inc(atT_ps, 1)

            def scores(i):
                at_least(pe, prob_ready, i - 1)
                if i < 4:
                    for j in range(2):
                        mm = pe.matmul(ps[:, i % 2, 256 * j:256 * (j + 1)], qT[:, CTX, 2 * i + j, :],
                                       kTz_ctx[:, i, :, :], start=True, stop=True)
                else:
                    mm = pe.matmul(ps[:, i % 2, :], qT[:, LAT, i - 4, :], kTz_lat[:, (i - 4) // 2, :, :],
                                   start=True, stop=True)
                mm.then_inc(score_ps, 1)

            def prob_transposes(i):
                pe.wait_ge(prob_ready, i + 1)
                at_least(pe, probT_ready, i - 1)
                for j in range(4):
                    mm = pe.transpose(ps[:, 2 + i % 2, j * P:(j + 1) * P], prob[:, i % 2, j * P:(j + 1) * P], ident)
                mm.then_inc(probT_ps, 1)

            def values(i):
                pe.wait_ge(probT_ready, i + 1)
                if i == 4:
                    pe.wait_ge(ha_ready, 1)
                for c in range(4 if i < 4 else 2):
                    hd = 4 * i + c if i < 4 else 2 * (i - 4) + c
                    out = ps[:, 4 + hd // 8, (hd % 8) * HD:(hd % 8 + 1) * HD]
                    v = ZAV + hd // 4 * HD
                    if i < 4:
                        mm = pe.matmul(out, probT[:, i % 2, c * P:(c + 1) * P], Z[:, CTX, v:v + HD], start=True, stop=True)
                    else:
                        o = 2 * c * P
                        pe.matmul(out, probT[:, i % 2, o:o + P], Z[:, LAT, v:v + HD], start=True, stop=False)
                        mm = pe.matmul(out, probT[:, i % 2, o + P:o + 2 * P], cache_v[:, v - ZAV:v - ZAV + HD],
                                       start=False, stop=True)
                mm.then_inc(pv_done, 1)

            gm_unit(2 * AHEAD - 1)
            pe.wait_ge(kT_copied, 3)
            pe.wait_ge(qT_copied, 4)
            for i in range(14):
                if i < 12:
                    scores(i)
                if 1 <= i <= 12:
                    prob_transposes(i - 1)
                if i >= 2:
                    values(i - 2)
                if i in (2, 3):
                    gm_unit(2 * AHEAD + i - 2)

            def blocks_T(at, done):
                for j in range(8):
                    if j == 6:
                        pe.wait_ge(sgm_ready, 1)
                    for b in range(2):
                        for g in range(GROUPS):
                            mm = pe.transpose(ps[:, j, b * TOK + g * P:b * TOK + (g + 1) * P], at(g, 2 * j + b), ident)
                    mm.then_inc(done, 1)

            pe.wait_ge(ha_ready, 2)
            pe.wait_ge(hm_ready, 1)
            blocks_T(lambda g, k: Z[:, g, ZV + k * P + k // 2:ZV + (k + 1) * P + k // 2] if k < 8 else Z[:, g, ZAQ + (k - 8) * P:ZAQ + (k - 7) * P],
                     hcT_ps)
            pe.wait_ge(hcT_lo_ready, 8)

            def merge(n, ux):
                if not isinstance(n, int):
                    pe.wait_ge(sgm_ready, n)
                    x_chunk(U_MERGE, ux, 0)
                at_least(pe, sga_ready, n)
                x_chunk(U_MERGE + 8, ux, 2)
                at_least(pe, gm_used, n)
                for k in range(4):
                    unit(U_MERGE + 16 + k, ux, hcT_hi, hcT_lo, 2 * k, 4, k == 0, k == 3)
                at_least(pe, mix_ready, n)
                for k in range(4):
                    unit(U_MERGE + 20 + k, ux, hcT_hi, hcT_lo, 8 + 2 * k, 6, k == 0, k == 3)

            merge(0, 0)
            with pe.Fori(1, NCH) as n:
                merge(n, n * 24)
            pe.wait_ge(mix_ready, NCH)
            blocks_T(lambda g, k: mix[:, g, k * P:(k + 1) * P], mixT_ps)
            for n in range(NCH):
                if n >= 2:
                    pe.wait_ge(x_updated, NCH + n - 1)
                for k in range(8):
                    if n == 0:
                        pe.wait_ge(mixT_lo_ready, min(k + 2, 8))
                    unit(U_OUT + 8 * n + k, 0, xT_hi, xT_lo, 2 * k, 2 * (n % 2), k == 0, k == 7)
            norm(2)
            ffn(1, U_F2, 2)

        @blk.scalar
        def _(act):
            chain = Chain(act, act_chain)

            def split(us, ux):
                if isinstance(ux, int) and us + ux >= U_END:
                    return
                slot = (us // 2) % RAW
                if us % 2 == 0:
                    act.wait_ge(raw_landed[slot], 16 * (us // 2 // RAW + 1) + ux * 2)
                at_least(act, units_done, us + ux - SPL + 1)
                half = us % 2
                act.copy(w_hi[:, us % SPL, :, :], raw_w[:, slot, 2 * half:2 * half + 2, :]).then_inc(hi_ready, 1)

            def ada_load(c, par, tiles=range(4)):
                src = I["ada_b"][0:1, bass.ds(c * CH, CH)].broadcast_to([GROUPS, CH])
                if 0 in tiles:
                    at_least(act, ada_rows_done, c - 1)
                    act.dma_start(ada_bias[0:GROUPS, par, :], src).then_inc(bias_landed[par], 16)
                for q in tiles:
                    w = I["ada_w"][0].rearrange("(q k p) n -> q p k n", k=4, p=P)[q]
                    at_least(act, ada_used, 4 * c + q - 3)
                    act.dma_start(ada_w_sb[:, q, :, :], w[:, :, bass.ds(c * CH, CH)]).then_inc(ada_landed[q], 16)

            def sumsq(s, n):
                at_least(act, x_updated, NCH * (s - 1) + n + 1)
                at_least(act, sumsq_ready, 2 * (NCH * s + n) if n else 0)
                for g in range(GROUPS):
                    act.activation(sg[:, g, :], x[:, g, n * CH:(n + 1) * CH], ACT.Square,
                                   accum_out=small[:, 4 * g + n:4 * g + n + 1]).then_inc(sumsq_ready, 1)

            def root(s):
                act.wait_ge(var_ready, s + 1)
                act.activation(small[:, 12:14], small[:, 10:12], ACT.Sqrt).then_inc(root_ready, 1)

            def norm(s, sh):
                act.wait_ge(acol_ready, s + 1)
                for j in range(8):
                    if j % 2:
                        act.wait_ge(norm_ps, 8 * s + j + 1)
                        for b in range(2):
                            for g in range(GROUPS):
                                k = 2 * j + b
                                ins = act.activation(xm[:, k, g * P:(g + 1) * P], ps[:, j, b * TOK + g * P:b * TOK + (g + 1) * P],
                                                     ACT.Identity, scale=acol[:, k, g:g + 1],
                                                     bias=adacols[:, sh * KD + k, g:g + 1])
                        ins.then_inc(xm_act, 1)
                        act.wait_ge(xm_act, 4 * s + j // 2 + 1)
                    else:
                        act.wait_ge(xm_ready, 4 * s + j // 2 + 1)
                    act.copy(xT_hi[:, 2 * j:2 * j + 2, :], xm[:, 2 * j:2 * j + 2, :]).then_inc(xT_hi_ready, 1)

            def ffn(f, u0):
                def hT_hi_of(i):
                    act.wait_ge(hT_ps, FCH * f + i + 1)
                    act.copy(hT_hi[:].rearrange("p (a b) t -> p a (b t)", a=2), ps[:, 4:6, :]).then_inc(hT_hi_ready, 1)

                def ffn_in(i, us, ux, ada=None, last=False):
                    first = isinstance(i, int) and i == 0
                    for k in range(16):
                        split(us + k + AHEAD, ux)
                        if k == 0 and not first:
                            hT_hi_of(i - 1)
                        if ada is not None and k == 2:
                            ada_load(ada + 1, 1)
                        if ada is not None and k == 14:
                            ada_load(ada + 2, 0, range(2) if last else range(4))
                        if k == 7:
                            act.wait_ge(units_done, us + ux + 8)
                            if not first:
                                act.wait_ge(h_done, FCH * f + i)
                            act.activation(sg[:], ps[:, 0:2, :], ACT.Silu).then_inc(silu_done, 1)

                def step(i, ux, last=False):
                    ffn_in(i, u0 + 16, ux, 2 * i + ADA_PRE - 2 if f == 0 else None, last)
                    for k in range(8):
                        split(u0 + 32 + k + AHEAD, ux)

                ffn_in(0, u0, 0)
                with act.Fori(1, FCH - 1) as i:
                    step(i, (i - 1) * 24)
                step(FCH - 1, (FCH - 2) * 24, True)
                for k in range(8):
                    split(u0 + 16 + 24 * (FCH - 1) + k + AHEAD, 0)
                    if k == 0:
                        hT_hi_of(FCH - 1)
                        act.wait_ge(h_done, FCH * f + FCH)
                    if f == 0 and k in (4, 6):
                        sumsq(1, k // 2 - 2)

            act.wait_ge(bias_zeroed, 1)
            ada_load(0, 0)
            act.wait_ge(cols_ps, 1)
            act.activation(ctile[:, :, 0:GROUPS].rearrange("p k g -> p g k"),
                           ps[:, 0, 0:GROUPS * KD].rearrange("p (g k) -> p g k", g=GROUPS),
                           ACT.Silu).then_inc(cond_silu, 1)
            for c in range(1, 6):
                ada_load(c, c % 2)
            act.wait_ge(x_landed, 32)
            for n in range(NCH):
                sumsq(0, n)
            root(0)
            for c in range(6, ADA_PRE):
                ada_load(c, c % 2)
            for u in range(AHEAD):
                split(u, 0)
            ada_load(ADA_PRE, 0)
            norm(0, SH1)
            ffn(0, U_F1)
            sumsq(1, 2)
            sumsq(1, 3)
            root(1)
            ada_load(ADA_PRE + 2 * (FCH - 1), 0, range(2, 4))

            norm(1, SH2)
            act.wait_ge(wg_landed, 16)
            act.copy(wg[:, :, 0, :], wg_raw[:]).then_inc(wg_hi_ready, 1)

            def z_pair(c, ux, last=False):
                for m in range(2):
                    for k in range(8):
                        split(U_IN + 8 * m + k + AHEAD, ux)
                        if k == 4 and not (last and m):
                            ada_load(c + m + 4 * G2 + 9, 1 - m)
                        if k == 7:
                            act.wait_ge(units_done, U_IN + 8 * m + 8 + ux)
                            src = ps[:, 2 * m:2 * m + 2, :]
                            if c == ZV // CH:
                                o = ZV + 2 * m * VW
                                dst = Z[:, :, o:o + 2 * VW].rearrange("p g (h v) -> p g h v", h=2)[:, :, :, 0:MV]
                                src = src.rearrange("p g (h v) -> p g h v", h=2)
                            else:
                                o = (c + m) * CH + (MH if c > ZV // CH else 0)
                                dst = Z[:, :, o:o + CH]
                            act.activation(dst, src, ACT.Sigmoid if c == 4 else ACT.Copy).then_inc(z_copied, 1)

            for c in range(0, 8, 2):
                z_pair(c, 8 * c, c == 6)
            for k in range(8):
                split(U_IN + 64 + k + AHEAD, 0)
            act.wait_ge(units_done, U_MERGE)
            act.copy(Z[:, :, ZW - CH:ZW], ps[:, 0:2, :]).then_inc(z_copied, 1)

            act.wait_ge(absf_ready, 1)
            chain(act.activation(exp_negm[:], absf[:], ACT.Exp, scale=-1.0))
            act.activation(den[:], exp_negm[:], ACT.Ln, bias=1.0).then_inc(softplus_ready, 1)
            for n in range(2):
                act.wait_ge(qkT_ps, n + 1)
                act.copy(qkT[:, n, :, :].rearrange("p h t -> p (h t)"), ps[:, n, :]).then_inc(qkT_copied_act, 1)
            act.wait_ge(qk_var, 1)
            act.activation(stat[:, 1, :], stat[:, 0, :], ACT.Sqrt).then_inc(qk_root, 1)
            act.wait_ge(mt_ready, 1)
            act.activation(exp_negm[:], mt[:].rearrange("p d c -> p (d c)"), ACT.Exp, scale=-1.0).then_inc(exps_ready, 1)
            act.wait_ge(wk_arg, 2)
            act.activation(decay[:], decay[:], ACT.Exp).then_inc(exps_ready, 1)
            act.activation(wk[:], wk[:], ACT.Exp).then_inc(wk_ready, 1)
            for n in range(2):
                act.wait_ge(CT_ps, n + 1)
                act.copy(CT[:, 2 * n:2 * n + 2, 0:MV], ps[:, 2 + n, :].rearrange("p (a v) -> p a v", a=2)).then_inc(CT_copied_act, 1)

            def decays_of(i):
                d, g = i // 2, i % 2
                act.wait_ge(mb_ps, i + 1)
                at_least(act, sT_ready, i - 1)
                for hd in range(MH):
                    ins = act.activation(decays[:, i % 2, hd, :], ps[:, 2 + i % 2, hd * P:(hd + 1) * P], ACT.Exp,
                                         bias=apad[:, d, g * MH + hd:g * MH + hd + 1], scale=-1.0)
                ins.then_inc(decays_ready, 1)

            def sv_copy(i):
                if i == 0:
                    act.wait_ge(CT_ps, 4)
                for hd in range(MH):
                    n = 4 * i + hd
                    act.wait_ge(sv_ps, n + 1)
                    act.copy(num[:, n, :], ps[:, 4 + n % 2, 0:MV + 1]).then_inc(sv_copied, 1)

            for i in range(5):
                if i < 4:
                    decays_of(i)
                if 1 <= i < 4:
                    split(U_MERGE + AHEAD + i - 1, 0)
                if i:
                    sv_copy(i - 1)
            for n in range(2):
                act.wait_ge(state_ps, n + 1)
                act.wait_ge(inter_added, 8)
                act.copy(c_new[:, 0, 4 * n:4 * n + 4, :].rearrange("p a k -> p (a k)"), ps[:, 2 + n, :]).then_inc(state_copied_act, 1)
            act.wait_ge(den_ready, 1)
            for c in range(GROUPS * MH):
                act.activation(num[:, c, 0:MV], num[:, c, 0:MV], ACT.Copy, scale=den[:, c:c + 1]).then_inc(fw_ready, 1)
            for c in range(GROUPS * MH):
                g, o = c // MH, ZV + (c % MH) * VW
                act.wait_ge(h_summed, c + 1)
                act.activation(num[:, c, 0:MV], Z[:, g, o:o + MV], ACT.Square, accum_out=hstat[:, 0, c:c + 1]).then_inc(h_squared, 1)
            act.wait_ge(h_var, 1)
            act.activation(hstat[:, 2, :], hstat[:, 1, :], ACT.Sqrt).then_inc(h_root, 1)

            for n in range(4):
                act.wait_ge(atT_ps, n + 1)
                act.copy(qT[:, n // 2, 4 * (n % 2):4 * (n % 2) + 4, :].rearrange("p a t -> p (a t)"),
                         ps[:, n, :]).then_inc(qT_copied, 1)

            for i in range(12):
                act.wait_ge(neg_max_ready, i + 1)
                at_least(act, probT_ps, i - 1)
                heads, keys = (4, P) if i < 4 else (2, 2 * P)
                for c in range(heads):
                    col = 4 * i + c if i < 4 else AH + 2 * (i - 4) + c
                    ins = act.activation(prob[:, i % 2, c * keys:(c + 1) * keys], ps[:, i % 2, c * keys:(c + 1) * keys],
                                         ACT.Exp, bias=neg_max[:, col:col + 1], accum_out=row_sum[:, col:col + 1])
                ins.then_inc(prob_ready, 1)
                if i < 8 - AHEAD:
                    split(U_MERGE + 2 * AHEAD + i, 0)
                if i in (5, 11):
                    act.wait_ge(sink_arg, i // 6 + 1)
                    act.activation(stat[:, 1, 0:AH], stat[:, 0, 0:AH], ACT.Exp).then_inc(sink_exp, 1)
            act.wait_ge(units_done, U_MERGE + 8)
            act.activation(sgm[:], ps[:, 6:8, :], ACT.Sigmoid).then_inc(sgm_ready, 1)

            def blocks_hi(hi, src_ps, done):
                for j in range(8):
                    act.wait_ge(src_ps, j + 1)
                    act.copy(hi[:, 2 * j:2 * j + 2, :].rearrange("p a t -> p (a t)"), ps[:, j, :]).then_inc(done, 1)

            blocks_hi(hcT_hi, hcT_ps, hcT_hi_ready)

            def merge(n, ux):
                for k in range(8 if isinstance(n, int) else 0, 24):
                    split(U_MERGE + k + AHEAD, ux)
                    if k == 7:
                        act.wait_ge(units_done, U_MERGE + 8 + ux)
                        at_least(act, mix_ready, n)
                        act.activation(sgm[:], ps[:, 0:2, :], ACT.Sigmoid).then_inc(sgm_ready, 1)
                    if k == 15:
                        act.wait_ge(units_done, U_MERGE + 16 + ux)
                        act.activation(sga[:], ps[:, 2:4, :], ACT.Sigmoid).then_inc(sga_ready, 1)

            merge(0, 0)
            with act.Fori(1, NCH) as n:
                merge(n, n * 24)
            blocks_hi(xT_hi, mixT_ps, mixT_hi_ready)
            for k in range(8 * NCH):
                split(U_OUT + k + AHEAD, 0)
                if k % 8 == 4 and k > 8:
                    sumsq(2, k // 8 - 1)
            sumsq(2, 3)
            root(2)
            norm(2, SH3)
            ffn(1, U_F2)

        @blk.vector
        def _(dve):
            chain = Chain(dve, dve_chain)

            def split(us, ux):
                if isinstance(ux, int) and us + ux >= U_END:
                    return
                slot, half = (us // 2) % RAW, us % 2
                dve.wait_ge(hi_ready, us + ux + 1)
                dve.tensor_tensor(w_lo[:, us % SPL, :, :], raw_w[:, slot, 2 * half:2 * half + 2, :],
                                  w_hi[:, us % SPL, :, :].bitcast(F32), ALU.subtract).then_inc(lo_ready, 1)

            def ada_rows(c, par, uses):
                dve.wait_ge(ada_used, 4 * c + 4)
                dve.wait_ge(bias_landed[par], uses)
                at_least(dve, ada_T_done, c)
                dve.tensor_tensor(ada_rows_sb[:], ps[:, 6, :], ada_bias[:, par, :], ALU.add).then_inc(ada_rows_done, 1)

            def gates_copy(vecs, n):
                dve.wait_ge(gate_rows_ps, n)
                dve.tensor_copy(gate_rows[:, 0:len(vecs), :], ps[0:2 * KD, 7, 0:P * len(vecs)].rearrange("k (v p) -> k v p", p=P)
                                ).then_inc(gate_rows_ready, 1)

            def ada_blk(c):
                dve.wait_ge(ada_sel_done, c + 1)
                dve.tensor_copy(ada_rows_sb[:, 0:P], ps[:, 7, 0:P]).then_inc(ada_blk_ready, 1)

            def ada_cols(c):
                dve.wait_ge(ada_T_done, c + 1)
                dve.tensor_copy(adacols[:, bass.ds(4 * c, 4), :],
                                ps[:, 7, P:2 * P].rearrange("p (b x) -> p b x", x=32)[:, :, 0:GROUPS]).then_inc(ada_cols_done, 1)

            def scale(s, sc):
                dve.wait_ge(ada_cols_done, 4 * (sc + 1))
                dve.scalar_tensor_tensor(
                    acol[:], adacols[:, sc * KD:(sc + 1) * KD, :], 1.0,
                    normw[:, s, :].unsqueeze(2).to_broadcast([P, KD, GROUPS]), ALU.add, ALU.mult).then_inc(acol_ready, 1)

            def rms(s):
                dve.wait_ge(sumsq_ready, 2 * NCH * (s + 1))
                chain(dve.tensor_reduce(small[:, 8:10], small[:, 0:8].rearrange("p (g n) -> p g n", g=GROUPS), AX.X, ALU.add))
                dve.tensor_scalar(small[:, 10:12], small[:, 8:10], 1.0 / D, EPS, ALU.mult, ALU.add).then_inc(var_ready, 1)
                dve.wait_ge(root_ready, s + 1)
                chain(dve.reciprocal(small[:, 14:16], small[:, 12:14]))
                for g in range(GROUPS):
                    ins = dve.tensor_scalar(diag[:, g, :], ident, small[:, 14 + g:15 + g], None, ALU.mult)
                ins.then_inc(diag_ready, 1)

            def norm(s, sh):
                dve.wait_ge(acol_ready, s + 1)

                def modulate(j):
                    dve.wait_ge(norm_ps, 8 * s + j + 1)
                    for b in range(2):
                        for g in range(GROUPS):
                            k = 2 * j + b
                            ins = dve.tensor_scalar(xm[:, k, g * P:(g + 1) * P], ps[:, j, b * TOK + g * P:b * TOK + (g + 1) * P],
                                                    acol[:, k, g:g + 1], adacols[:, sh * KD + k, g:g + 1], ALU.mult, ALU.add)
                    ins.then_inc(xm_ready, 1)

                def low(j):
                    dve.wait_ge(xT_hi_ready, 8 * s + j + 1)
                    dve.tensor_tensor(xT_lo[:, 2 * j:2 * j + 2, :], xm[:, 2 * j:2 * j + 2, :],
                                      xT_hi[:, 2 * j:2 * j + 2, :].bitcast(F32), ALU.subtract).then_inc(xT_lo_ready, 1)

                modulate(0)
                for j in range(8):
                    if s == 0 and j < AHEAD:
                        split(j, 0)
                    if j % 2 == 0 and j < 6:
                        modulate(j + 2)
                    low(j)

            def ffn(f, u0):
                def hT_lo_of(i):
                    dve.wait_ge(hT_hi_ready, FCH * f + i + 1)
                    dve.tensor_tensor(hT_lo[:].rearrange("p (a b) t -> p a (b t)", a=2), ps[:, 4:6, :],
                                      hT_hi[:].bitcast(F32).rearrange("p (a b) t -> p a (b t)", a=2),
                                      ALU.subtract).then_inc(hT_lo_ready, 1)

                def ffn_in(i, us, ux, ada=None):
                    for k in range(16):
                        split(us + k + AHEAD, ux)
                        if k == 0 and not isinstance(i, int):
                            hT_lo_of(i - 1)
                        if ada is not None:
                            if k == 1:
                                ada_rows(ada, 0, 8 * ada + 16)
                            if k == 3:
                                ada_blk(ada)
                            if k == 5:
                                ada_cols(ada)
                            if k == 7:
                                gates_copy((G1,), i)
                            if k == 13:
                                ada_rows(ada + 1, 1, 8 * ada + 16)
                            if k == 15:
                                ada_blk(ada + 1)
                        if k == 15:
                            dve.wait_ge(units_done, us + ux + 16)
                            dve.wait_ge(silu_done, FCH * f + i + 1)
                            if not isinstance(i, int):
                                dve.wait_ge(hT_ps, FCH * f + i)
                            dve.tensor_tensor(h[:], sg[:], ps[:, 2:4, :], ALU.mult).then_inc(h_done, 1)
                            if ada is not None:
                                ada_cols(ada + 1)

                def ffn_out(j, us, ux, epilogue=False):

                    def add_acc(n):
                        c = slice(n * CH, (n + 1) * CH)
                        if n == 0:
                            dve.wait_ge(gate_landed, 32 * (2 * f + 1))
                            dve.wait_ge(acc_done, 45 * f + 4 * j + 1)
                        chain(dve.tensor_tensor(acc[:, :, c], acc[:, :, c], gate_bc[:, :, c], ALU.mult))
                        chain(dve.scalar_tensor_tensor(x[:, :, c], acc[:, :, c], 0.5, x[:, :, c], ALU.mult, ALU.add))

                    for k in range(8):
                        split(us + k + AHEAD, ux)
                        if k == 0 and epilogue:
                            hT_lo_of(j)
                            for n in range(2):
                                add_acc(n)
                        if k in (2, 4) and epilogue:
                            add_acc(k // 2 + 1)
                        if k % 2:
                            n = k // 2
                            c = slice(n * CH, (n + 1) * CH)
                            banks = 4 if n % 2 == 0 else 2
                            dve.wait_ge(units_done, us + ux + k + 1)
                            if not epilogue:
                                dve.wait_ge(acc_done, 45 * f + 4 * j + n + 1)
                                dve.tensor_tensor(acc[:, :, c], acc[:, :, c], ps[:, banks:banks + 2, :], ALU.add).then_inc(acc_done, 1)
                            else:
                                dve.tensor_tensor(acc[:, :, c], ps[:, banks:banks + 2, :], gate_bc[:, :, c], ALU.mult).then_inc(acc_done, 1)
                                dve.wait_ge(acc_done, 45 * f + 4 * j + n + 2)
                                dve.scalar_tensor_tensor(x[:, :, c], acc[:, :, c], 0.5, x[:, :, c], ALU.mult, ALU.add).then_inc(x_updated, 1)

                ffn_in(0, u0, 0)
                with dve.Fori(1, FCH) as i:
                    ffn_in(i, u0 + 16, (i - 1) * 24, 2 * i + ADA_PRE - 2 if f == 0 else None)
                    ffn_out(i - 1, u0 + 32, (i - 1) * 24)
                ffn_out(FCH - 1, u0 + 16 + 24 * (FCH - 1), 0, True)

            dve.memset(ctile[:], 0.0)
            dve.memset(adacols[:, G1 * KD:(G1 + 1) * KD, :], 0.0)
            dve.memset(ada_bias[:], 0.0).then_inc(bias_zeroed, 1)
            dve.memset(m0_row[:], 0.0)
            dve.memset(apad[:], 0.0)
            for t in scan:
                ins = dve.memset(t[:], NEG)
            ins.then_inc(zeroed, 1)
            dve.wait_ge(cols_ps, 1)
            dve.wait_ge(cond_silu, 1)
            chain(dve.tensor_copy(normw[:].rearrange("p s k -> p (s k)"), ps[:, 0, 32:80]))
            for c in range(ADA_PRE):
                ada_rows(c, c % 2, 16 * (c // 2 + 1))
                ada_blk(c)
                ada_cols(c)
                if c == 5:
                    rms(0)
            scale(0, SC1)
            norm(0, SH1)
            ffn(0, U_F1)
            scale(1, SC2)
            rms(1)

            norm(1, SH2)
            dve.wait_ge(xT_lo_ready, 16)
            dve.memset(Z[:, :, ZV:ZO].rearrange("p g (h v) -> p g h v", h=MH)[:, :, :, MV:VW], 1.0).then_inc(ones_ready, 1)
            dve.wait_ge(wg_hi_ready, 1)
            dve.tensor_tensor(wg[:, :, 1, :], wg_raw[:], wg[:, :, 0, :].bitcast(F32), ALU.subtract).then_inc(wg_ready, 1)

            def z_pair(c, ux):
                for m in range(2):
                    a = c + m + 4 * G2 + 8
                    for k in range(8):
                        split(U_IN + 8 * m + k + AHEAD, ux)
                        if k == 4:
                            ada_rows(a, m, 8 * c + 16 * (2 * G2 + 5))
                        if k == 6:
                            ada_blk(a)
                        if k == 7:
                            ada_cols(a)

            z_pair(0, 0)
            dve.wait_ge(gT_ps, 1)
            dve.tensor_copy(gT[:], ps[0:2 * NG, 4, 0:TOK]).then_inc(gT_ready, 1)
            dve.wait_ge(misc_landed, 16 * 11)
            dve.wait_ge(gates_ps, 1)
            chain(dve.tensor_tensor(gates[:], ps[:, 5, 0:GROUPS * NG].rearrange("p (g n) -> p g n", g=GROUPS),
                                    gateb[:].unsqueeze(1).to_broadcast([P, GROUPS, NG]), ALU.add))
            gate = gates[:].rearrange("p g (d i h) -> p i d g h", d=2, i=2)
            i_pre, f_pre = gate[:, 0], gate[:, 1]

            def by_dgh(t):
                return t.rearrange("p d (g h) -> p d g h", g=GROUPS)

            absf_v = absf[:].rearrange("p (d g h) -> p d g h", d=2, g=GROUPS)
            for d in range(2):
                ins = dve.scalar_tensor_tensor(absf_v[:, d], f_pre[:, d], -1.0, f_pre[:, d], ALU.mult, ALU.max)
            ins.then_inc(absf_ready, 1)
            with dve.Fori(1, 4) as i:
                z_pair(2 * i, i * 16)
            gates_copy((G2, G3), FCH)
            chain(dve.tensor_scalar(qk_w[:, 0, :], qk_w[:, 0, :], HD ** -0.5, None, ALU.mult))
            HN = AH + AKV
            Zqk = Z[:, :, ZAQ:ZAV]

            def head_squares(g, h0, n):
                z = Zqk[:, g, h0 * HD:(h0 + n) * HD].rearrange("p (h d) -> p h d", d=HD)
                chain(dve.tensor_tensor(head_tmp[:, 0:n, :], z, z, ALU.mult))
                chain(dve.tensor_reduce(stat[:, 0, HN * g + h0:HN * g + h0 + n], head_tmp[:, 0:n, :], AX.X, ALU.add))

            for k in range(8):
                split(U_IN + 64 + k + AHEAD, 0)
                if k in (2, 4):
                    dve.wait_ge(zo_ready, 1)
                    dve.wait_ge(z_copied, 8)
                    head_squares(k // 2 - 1, 0, AH)

            dve.wait_ge(softplus_ready, 1)
            den_v = den[:].rearrange("p (d g h) -> p d g h", d=2, g=GROUPS)
            for d in range(2):
                ins = dve.scalar_tensor_tensor(by_dgh(lf[:])[:, d], f_pre[:, d], 0.0, den_v[:, d], ALU.min, ALU.subtract)
            ins.then_inc(lf_ready, 1)
            dve.wait_ge(b_ps, 1)
            b_v = ps[:, 4, 0:NC].rearrange("p (d g h) -> p d g h", d=2, g=GROUPS)
            dve.tensor_copy(bcol[:].rearrange("p d c -> p (d c)"), ps[:, 4, 0:NC])
            for d in range(2):
                ins = dve.tensor_tensor(by_dgh(apad[:, :, 0:GROUPS * MH])[:, d], i_pre[:, d], b_v[:, d], ALU.subtract)
            ins.then_inc(a_ready, 1)
            dve.wait_ge(aT_ps, 1)
            H = P // 2
            dve.wait_ge(z_copied, ZCH)
            for g in range(GROUPS):
                head_squares(g, AH, AKV)
            dve.tensor_scalar(stat[:, 0, :], stat[:, 0, :], 1.0 / HD, EPS, ALU.mult, ALU.add).then_inc(qk_var, 1)
            chain(dve.tensor_scalar(scan[0][:, H:H + P], ps[0:40, 5, 0:P], m0_row[:, 0:1], None, ALU.max))
            for n in range(7):
                src, dst, s = scan[n % 2], scan[(n + 1) % 2], 1 << n
                for r, to in ((slice(0, 8), -s), (slice(32, 40), s)):
                    dve.tensor_tensor(dst[r, H:H + P], src[r, H:H + P], src[r, H + to:H + to + P], ALU.max).then_inc(scan_done, 1)
                dve.wait_ge(scan_done, 2 * (n + 1))
            for n in range(2, 4):
                dve.wait_ge(qkT_ps, n + 1)
                dve.tensor_copy(qkT[:, n, :, :].rearrange("p h t -> p (h t)"), ps[:, n, :]).then_inc(qkT_copied, 1)
            dve.wait_ge(qk_root, 1)
            dve.reciprocal(stat[:, 2, :], stat[:, 1, :]).then_inc(qk_rinv, 1)
            dve.wait_ge(mT_ps, 1)
            chain(dve.tensor_copy(mcol[:, 0, :], ps[:, 4, 0:8]), dve.tensor_copy(mcol[:, 1, :], ps[:, 4, 32:40]))
            dve.tensor_copy(CT[:, :, MV:MV + 1].rearrange("p n a -> p (n a)"), ps[:, 4, 40:40 + 2 * MH]).then_inc(CT_copied, 1)
            dve.tensor_tensor(decay[:], m0_bc[:], mcol[:, :, MH:2 * MH], ALU.subtract).then_inc(m_ready, 1)
            dve.tensor_tensor(mt[:], bcol[:], mcol[:], ALU.add).then_inc(mt_ready, 1)
            dve.wait_ge(m_last_ps, 1)
            for d in range(2):
                dve.tensor_tensor(wk[:, :, d], apad[:, d, 0:MH], ps[:, 5, 4 * d:4 * d + 4], ALU.subtract).then_inc(wk_arg, 1)
            for n in range(2, 4):
                dve.wait_ge(CT_ps, n + 1)
                dve.tensor_copy(CT[:, 2 * n:2 * n + 2, 0:MV], ps[:, 2 + n, :].rearrange("p (a v) -> p a v", a=2)).then_inc(CT_copied, 1)
            dve.wait_ge(exps_ready, 2)
            chain(dve.tensor_scalar(decay[:], decay[:], MQK ** -0.5, None, ALU.mult))
            for i in range(4):
                d, g = i // 2, i % 2
                dve.wait_ge(decays_ready, i + 1)
                dve.wait_ge(qk_ps, g + 1)
                at_least(dve, sv_ps, 4 * (i - 1))
                dve.scalar_tensor_tensor(sT[:, i % 2, :, :].rearrange("p h t -> p (h t)"), ps[:, g, :], MQK ** -0.5,
                                         decays[:, i % 2, :, :].rearrange("p h t -> p (h t)"),
                                         ALU.mult, ALU.mult).then_inc(sT_ready, 1)
                if i:
                    split(U_MERGE + AHEAD + i - 1, 0)
            for n in range(2 * MH):
                d, hd = n // MH, n % MH
                col = d * GROUPS * MH + MH + hd
                dve.wait_ge(inter_ps, n + 1)
                dve.wait_ge(sv_copied, col + 1)
                dve.scalar_tensor_tensor(num[:, col, :], ps[:, 2 + n % 2, 0:MV + 1], decay[:, d, hd:hd + 1],
                                         num[:, col, :], ALU.mult, ALU.add).then_inc(inter_added, 1)
            dve.wait_ge(wk_ready, 1)
            dve.wait_ge(sv_ps, 16)
            for d in range(2):
                dve.tensor_tensor(v_wk[:, d, :, :], Z[:, CTX, ZV:ZO].rearrange("p (h v) -> p h v", h=MH)[:, :, 0:MV],
                                  wk[:, :, d:d + 1].to_broadcast([P, MH, MV]), ALU.mult).then_inc(v_wk_ready, 1)
            den_col = num[:, :, MV:MV + 1].rearrange("p c a -> p (c a)")
            dve.wait_ge(inter_added, 8)
            dve.wait_ge(exps_ready, 1)
            chain(dve.scalar_tensor_tensor(den[:], den_col, -1.0, den_col, ALU.mult, ALU.max))
            chain(dve.tensor_tensor(den[:], den[:], exp_negm[:], ALU.max))
            dve.reciprocal(den[:], den[:]).then_inc(den_ready, 1)
            for n in range(2):
                dve.wait_ge(state_ps, 3 + n)
                dve.tensor_copy(c_new[:, 1, 4 * n:4 * n + 4, :].rearrange("p a k -> p (a k)"), ps[:, 4 + n, :]).then_inc(state_copied, 1)
            dve.wait_ge(state_ps, 5)
            dve.tensor_copy(n_new[:], ps[0:2, 0, :]).then_inc(state_copied, 1)
            dve.wait_ge(den_ready, 1)
            for c in range(GROUPS * MH):
                g, o = c // MH, ZV + (c % MH) * VW
                dve.wait_ge(fw_ready, c + 1)
                dve.scalar_tensor_tensor(Z[:, g, o:o + MV], num[:, 8 + c, 0:MV], den[:, 8 + c:9 + c], num[:, c, 0:MV],
                                         ALU.mult, ALU.add).then_inc(h_summed, 1)
            dve.wait_ge(h_squared, GROUPS * MH)
            dve.tensor_scalar(hstat[:, 1, :], hstat[:, 0, :], 1.0 / MV, EPS, ALU.mult, ALU.add).then_inc(h_var, 1)
            dve.wait_ge(h_root, 1)
            chain(dve.reciprocal(hstat[:, 3, :], hstat[:, 2, :]))
            for c in range(GROUPS * MH):
                g, o, v = c // MH, (c % MH) * MV, ZV + (c % MH) * VW
                zh = Z[:, g, v:v + MV]
                ins = dve.scalar_tensor_tensor(zh, zh, hstat[:, 3, c:c + 1], Z[:, g, ZO + o:ZO + o + MV], ALU.mult, ALU.mult)
            ins.then_inc(hm_ready, 1)

            dve.wait_ge(rope_done, 1)
            dve.wait_ge(hm_ready, 1)
            for n, src in enumerate((Z[:, CTX, ZAK:ZAV], Z[:, LAT, ZAK:ZAV], cache_k[:])):
                dve.tensor_copy(k_dup[:, n, :, :, :], src.rearrange("p (k d) -> p k d", d=HD).unsqueeze(2).to_broadcast([P, AKV, 2, HD])
                                ).then_inc(k_dup_ready, 1)
            dve.wait_ge(kT_zeroed, 2)
            for n, (dst, o) in enumerate(((kTz_ctx, 0), (kTz_lat, 0), (kTz_lat, P))):
                dve.wait_ge(atT_ps, 5 + n)
                for a in range(2):
                    r = slice(64 * a, 64 * a + 64)
                    ins = dve.tensor_copy(dst[r, :, a, o:o + P], ps[r, n, :].rearrange("p (k s) -> p k s", k=AKV))
                ins.then_inc(kT_copied, 1)

            def maxima(i):
                heads = 4 if i < 4 else 2
                col = 4 * i if i < 4 else AH + 2 * (i - 4)
                mx = neg_max[:, col:col + heads]
                dve.wait_ge(score_ps, i + 1)
                chain(dve.tensor_reduce(mx, ps[:, i % 2, :].rearrange("p (h s) -> p h s", h=heads), AX.X, ALU.max))
                chain(dve.tensor_tensor(mx, mx, sink[:, col % AH:col % AH + heads], ALU.max))
                dve.tensor_scalar(mx, mx, -1.0, None, ALU.mult).then_inc(neg_max_ready, 1)

            def probT_copy(i):
                dve.wait_ge(probT_ps, i + 1)
                at_least(dve, pv_done, i - 1)
                dve.tensor_copy(probT[:, i % 2, :], ps[:, 2 + i % 2, :]).then_inc(probT_ready, 1)

            def normalised(g):
                dve.tensor_tensor(Z[:, g, ZAQ:ZAK].rearrange("p (h d) -> p h d", d=HD),
                                  ps[:, 4:6, :].rearrange("p a (h d) -> p (a h) d", d=HD),
                                  stat[:, 2, 0:AH].unsqueeze(2).to_broadcast([P, AH, HD]), ALU.mult).then_inc(ha_ready, 1)

            def sums(g):
                s = slice(AH * g, AH * (g + 1))
                dve.tensor_tensor(stat[:, 0, 0:AH], sink[:], neg_max[:, s], ALU.add).then_inc(sink_arg, 1)
                dve.wait_ge(sink_exp, g + 1)
                chain(dve.tensor_tensor(stat[:, 2, 0:AH], stat[:, 1, 0:AH], row_sum[:, s], ALU.add))
                chain(dve.reciprocal(stat[:, 2, 0:AH], stat[:, 2, 0:AH]))

            for i in range(13):
                if i < 12:
                    maxima(i)
                if i:
                    probT_copy(i - 1)
                if 1 <= i <= 8 - AHEAD:
                    split(U_MERGE + 2 * AHEAD + i - 1, 0)
                if i == 5:
                    dve.wait_ge(neg_max_ready, 4)
                    sums(CTX)
                    dve.wait_ge(pv_done, 4)
                    normalised(CTX)
            dve.wait_ge(ha_ready, 1)
            sums(LAT)
            dve.wait_ge(pv_done, 12)
            normalised(LAT)

            def blocks_lo(lo, hi, hi_done, done):
                for j in range(8):
                    dve.wait_ge(hi_done, j + 1)
                    dve.tensor_tensor(lo[:, 2 * j:2 * j + 2, :].rearrange("p a t -> p (a t)"), ps[:, j, :],
                                      hi[:, 2 * j:2 * j + 2, :].bitcast(F32).rearrange("p a t -> p (a t)"),
                                      ALU.subtract).then_inc(done, 1)

            blocks_lo(hcT_lo, hcT_hi, hcT_hi_ready, hcT_lo_ready)
            dve.wait_ge(kv_stored, 32)

            def merge(n, ux):
                for k in range(8 if isinstance(n, int) else 0, 24):
                    split(U_MERGE + k + AHEAD, ux)
                    if k == 19:
                        dve.wait_ge(units_done, U_MERGE + 20 + ux)
                        dve.wait_ge(sgm_ready, n + 1)
                        dve.tensor_tensor(sgm[:], sgm[:], ps[:, 4:6, :], ALU.mult).then_inc(gm_used, 1)
                    if k == 23:
                        dve.wait_ge(units_done, U_MERGE + 24 + ux)
                        dve.wait_ge(sga_ready, n + 1)
                        dve.tensor_tensor(sga[:], sga[:], ps[:, 6:8, :], ALU.mult).then_inc(ga_used, 1)
                        dve.wait_ge(ga_used, n + 1)
                        dve.tensor_tensor(mix[:, :, bass.ds(n * CH, CH)], sgm[:], sga[:], ALU.add).then_inc(mix_ready, 1)

            merge(0, 0)
            with dve.Fori(1, NCH) as n:
                merge(n, n * 24)
            blocks_lo(xT_lo, xT_hi, mixT_hi_ready, mixT_lo_ready)
            for n in range(NCH):
                for k in range(8):
                    split(U_OUT + 8 * n + k + AHEAD, 0)
                c = slice(n * CH, (n + 1) * CH)
                dve.wait_ge(units_done, U_OUT + 8 * n + 8)
                dve.wait_ge(gate_landed, 64)
                chain(dve.tensor_tensor(y_tmp[:], ps[:, 2 * (n % 2):2 * (n % 2) + 2, :], gate_bc[:, :, c], ALU.mult))
                dve.tensor_tensor(x[:, :, c], x[:, :, c], y_tmp[:], ALU.add).then_inc(x_updated, 1)
            scale(2, SC3)
            rms(2)
            norm(2, SH3)
            ffn(1, U_F2)


INPUTS = ["x_prompt", "x_sample", "cache_attn_k", "cache_attn_v", "state_mlstm_C", "state_mlstm_n", "state_mlstm_m",
          "c", "c_ctx", "ada_w", "ada_b", "norm_ffn1_w", "ffn1_wi", "ffn1_wo", "norm_mix_w", "w_in", "mlstm_gate_b",
          "mlstm_norm_w", "attn_q_norm_w", "attn_k_norm_w", "attn_sink", "w_proj_m", "w_proj_a", "w_out",
          "norm_ffn2_w", "ffn2_wi", "ffn2_wo"]
OUTPUTS = [("y_prompt", (1, P, D)), ("y_sample", (1, P, D)), ("new_attn_k", (1, 1, P, AKV, HD)),
           ("new_attn_v", (1, 1, P, AKV, HD)), ("new_mlstm_C", (1, 1, 2, MH, MV, MQK)),
           ("new_mlstm_n", (1, 1, 2, MH, MQK)), ("new_mlstm_m", (1, 1, 2, MH))]


def kernel(**inputs):
    import concourse.bacc as bacc
    from concourse.bass_utils import run_bass_kernel_spmd

    nc = bacc.Bacc("TRN2", target_bir_lowering=False, num_devices=1)
    arrays, I, O = {}, {}, {}
    for name in INPUTS + ["consts"]:
        a = np.ascontiguousarray(shape_constants() if name == "consts" else inputs[name])
        arrays[f"in_{name}"] = a
        I[name] = nc.dram_tensor(f"in_{name}", a.shape, F32, kind="ExternalInput").ap()
    for name, shape in OUTPUTS:
        O[name] = nc.dram_tensor(f"out_{name}", shape, F32, kind="ExternalOutput").ap()
    build(nc, I, O)
    r = run_bass_kernel_spmd(nc, [arrays], core_ids=[0])
    return tuple(r.results[0][f"out_{name}"] for name, _ in OUTPUTS)
```
